# Optimizing a Trainium2 kernel written in Bass

```python
import math
import jax, jax.numpy as jnp
from jax import lax
import numpy as np

D_MODEL = 1024
BATCH = 1
SEQ = 1024
DEPTH = 1
DEC_BATCH = 1
DEC_SEQ = 512
PAST_LEN = 128

D_FF = 2816
N_HEADS_A = 8
N_KV_A = 2
HEAD_DIM_A = 64
GROUP_A = N_HEADS_A // N_KV_A
WINDOW = 128
BLOCK = 128
N_HEADS_B = 8
Q_LORA = 256
KV_LORA = 128
NOPE_B = 64
ROPE_B = 32
QK_DIM_B = NOPE_B + ROPE_B
V_DIM_B = 64
ROPE_THETA = 10000.0
EPS = 1e-6
A_Q = N_HEADS_A * HEAD_DIM_A
A_KV = N_KV_A * HEAD_DIM_A
IN_WIDTH = A_Q + 2 * A_KV + Q_LORA + KV_LORA + ROPE_B
MIX_WIDTH = N_HEADS_A * HEAD_DIM_A + N_HEADS_B * V_DIM_B
N_MOD = 9

kernel_name = "hymba_swa_mla_macaron_adaln_encoder"

def rmsnorm(x, g):
    xf = x.astype(jnp.float32)
    y = xf * lax.rsqrt(jnp.mean(xf * xf, axis=-1, keepdims=True) + EPS)
    return (y * g.astype(jnp.float32)).astype(x.dtype)

def modulate(h, shift, scale):
    return h * (1 + scale[:, None, :]) + shift[:, None, :]

def rope(x):
    S, d = x.shape[1], x.shape[-1]
    pos = jnp.arange(S, dtype=jnp.float32)
    inv = ROPE_THETA ** (-jnp.arange(0, d, 2, dtype=jnp.float32) / d)
    ang = pos[:, None] * inv[None, :]
    cos = jnp.cos(ang)[None, :, None, :]
    sin = jnp.sin(ang)[None, :, None, :]
    xf = x.astype(jnp.float32)
    x1, x2 = xf[..., : d // 2], xf[..., d // 2:]
    out = jnp.concatenate([x1 * cos - x2 * sin, x2 * cos + x1 * sin], axis=-1)
    return out.astype(x.dtype)

def swiglu(h, wg, wu, wd):
    return (jax.nn.silu(h @ wg) * (h @ wu)) @ wd

def window_attention(q, k, v, sink):
    B, S, H, d = q.shape
    nb = S // BLOCK
    qb = q.reshape(B, nb, BLOCK, N_KV_A, GROUP_A, d)
    pad = ((0, 0), (BLOCK, BLOCK), (0, 0), (0, 0))
    kp = jnp.pad(k, pad).reshape(B, nb + 2, BLOCK, N_KV_A, d)
    vp = jnp.pad(v, pad).reshape(B, nb + 2, BLOCK, N_KV_A, d)
    kw = jnp.concatenate([kp[:, :-2], kp[:, 1:-1], kp[:, 2:]], axis=2)
    vw = jnp.concatenate([vp[:, :-2], vp[:, 1:-1], vp[:, 2:]], axis=2)
    s = jnp.einsum('bnqhgd,bnjhd->bnhgqj', qb, kw).astype(jnp.float32) / math.sqrt(d)
    qi = jnp.arange(BLOCK)[:, None]
    kj = jnp.arange(3 * BLOCK)[None, :]
    band = jnp.abs(kj - BLOCK - qi) <= WINDOW
    kpos = jnp.arange(nb)[:, None] * BLOCK + jnp.arange(3 * BLOCK)[None, :] - BLOCK
    inside = (kpos >= 0) & (kpos < S)
    mask = band[None, :, :] & inside[:, None, :]
    s = jnp.where(mask[None, :, None, None, :, :], s, -1e30)
    sk = sink.astype(jnp.float32).reshape(N_KV_A, GROUP_A)[None, None, :, :, None, None]
    m = jnp.maximum(jnp.max(s, axis=-1, keepdims=True), sk)
    p = jnp.exp(s - m)
    p = p / (jnp.sum(p, axis=-1, keepdims=True) + jnp.exp(sk - m))
    o = jnp.einsum('bnhgqj,bnjhd->bnqhgd', p.astype(v.dtype), vw)
    return o.reshape(B, S, H * d)

def dense_attention(q, k, v):
    B, S, H, dq = q.shape
    nb = S // BLOCK
    qb = q.reshape(B, nb, BLOCK, H, dq).transpose(1, 0, 2, 3, 4)
    scale = 1.0 / math.sqrt(dq)

    def one(qblk):
        s = jnp.einsum('bqhd,bkhd->bhqk', qblk, k).astype(jnp.float32) * scale
        p = jax.nn.softmax(s, axis=-1)
        return jnp.einsum('bhqk,bkhd->bqhd', p.astype(v.dtype), v)

    o = lax.map(one, qb)
    return o.transpose(1, 0, 2, 3, 4).reshape(B, S, H * v.shape[-1])

def token_mixing(h, w_in, swa_q_norm, swa_k_norm, swa_sink, mla_q_lora_norm, mla_w_uq,
                 mla_kv_lora_norm, mla_w_ukv, mla_q_norm, mla_k_norm, w_out):
    B, S, _ = h.shape
    z = h @ w_in
    cuts = np.cumsum([A_Q, A_KV, A_KV, Q_LORA, KV_LORA]).tolist()
    qa, ka, va, cq, ckv, kr = jnp.split(z, cuts, axis=-1)
    qa = rope(rmsnorm(qa.reshape(B, S, N_HEADS_A, HEAD_DIM_A), swa_q_norm))
    ka = rope(rmsnorm(ka.reshape(B, S, N_KV_A, HEAD_DIM_A), swa_k_norm))
    va = va.reshape(B, S, N_KV_A, HEAD_DIM_A)
    oa = window_attention(qa, ka, va, swa_sink)
    qb = (rmsnorm(cq, mla_q_lora_norm) @ mla_w_uq).reshape(B, S, N_HEADS_B, QK_DIM_B)
    kv = (rmsnorm(ckv, mla_kv_lora_norm) @ mla_w_ukv).reshape(B, S, N_HEADS_B, NOPE_B + V_DIM_B)
    k_nope, vb = kv[..., :NOPE_B], kv[..., NOPE_B:]
    k_rope = jnp.broadcast_to(kr[:, :, None, :], (B, S, N_HEADS_B, ROPE_B))
    kb = jnp.concatenate([k_nope, k_rope], axis=-1)
    qb = rmsnorm(qb, mla_q_norm)
    kb = rmsnorm(kb, mla_k_norm)
    qb = jnp.concatenate([qb[..., :NOPE_B], rope(qb[..., NOPE_B:])], axis=-1)
    kb = jnp.concatenate([kb[..., :NOPE_B], rope(kb[..., NOPE_B:])], axis=-1)
    ob = dense_attention(qb, kb, vb)
    return jnp.concatenate([oa, ob], axis=-1) @ w_out

def setup_inputs(seed: int = 0) -> dict:
    key = jax.random.key(seed)
    ks = jax.random.split(key, 32)
    f32 = jnp.float32

    def nrm(k, shape, std):
        return jax.random.normal(k, shape, f32) * std

    def gain(k, dim):
        return 1.0 + 0.02 * jax.random.normal(k, (DEPTH, dim), f32)

    L = DEPTH
    return {
        "x_prompt": nrm(ks[0], (BATCH, SEQ, D_MODEL), 1.0),
        "x_sample": nrm(ks[1], (DEC_BATCH, DEC_SEQ, D_MODEL), 1.0),
        "c_prompt": nrm(ks[2], (BATCH, D_MODEL), 1.0),
        "c_sample": nrm(ks[3], (DEC_BATCH, D_MODEL), 1.0),
        "ada_w": nrm(ks[4], (L, D_MODEL, N_MOD * D_MODEL), D_MODEL ** -0.5),
        "ada_b": nrm(ks[5], (L, N_MOD * D_MODEL), 0.02),
        "ffn1_norm": gain(ks[6], D_MODEL),
        "ffn1_wg": nrm(ks[7], (L, D_MODEL, D_FF), D_MODEL ** -0.5),
        "ffn1_wu": nrm(ks[8], (L, D_MODEL, D_FF), D_MODEL ** -0.5),
        "ffn1_wd": nrm(ks[9], (L, D_FF, D_MODEL), D_FF ** -0.5),
        "mix_norm": gain(ks[10], D_MODEL),
        "w_in": nrm(ks[11], (L, D_MODEL, IN_WIDTH), D_MODEL ** -0.5),
        "swa_q_norm": gain(ks[12], HEAD_DIM_A),
        "swa_k_norm": gain(ks[13], HEAD_DIM_A),
        "swa_sink": nrm(ks[14], (L, N_HEADS_A), 0.5),
        "mla_q_lora_norm": gain(ks[15], Q_LORA),
        "mla_w_uq": nrm(ks[16], (L, Q_LORA, N_HEADS_B * QK_DIM_B), Q_LORA ** -0.5),
        "mla_kv_lora_norm": gain(ks[17], KV_LORA),
        "mla_w_ukv": nrm(ks[18], (L, KV_LORA, N_HEADS_B * (NOPE_B + V_DIM_B)), KV_LORA ** -0.5),
        "mla_q_norm": gain(ks[19], QK_DIM_B),
        "mla_k_norm": gain(ks[20], QK_DIM_B),
        "w_out": nrm(ks[21], (L, MIX_WIDTH, D_MODEL), MIX_WIDTH ** -0.5),
        "ffn2_norm": gain(ks[22], D_MODEL),
        "ffn2_wg": nrm(ks[23], (L, D_MODEL, D_FF), D_MODEL ** -0.5),
        "ffn2_wu": nrm(ks[24], (L, D_MODEL, D_FF), D_MODEL ** -0.5),
        "ffn2_wd": nrm(ks[25], (L, D_FF, D_MODEL), D_FF ** -0.5),
        "final_norm": gain(ks[26], D_MODEL),
    }

def reference(x_prompt, x_sample, c_prompt, c_sample, ada_w, ada_b, ffn1_norm, ffn1_wg, ffn1_wu,
              ffn1_wd, mix_norm, w_in, swa_q_norm, swa_k_norm, swa_sink, mla_q_lora_norm, mla_w_uq,
              mla_kv_lora_norm, mla_w_ukv, mla_q_norm, mla_k_norm, w_out, ffn2_norm, ffn2_wg,
              ffn2_wu, ffn2_wd, final_norm):
    def trunk(x, c):
        for l in range(DEPTH):
            mod = jax.nn.silu(c) @ ada_w[l] + ada_b[l]
            sh1, sc1, g1, sh2, sc2, g2, sh3, sc3, g3 = jnp.split(mod, N_MOD, axis=-1)
            h = modulate(rmsnorm(x, ffn1_norm[l]), sh1, sc1)
            x = x + 0.5 * g1[:, None, :] * swiglu(h, ffn1_wg[l], ffn1_wu[l], ffn1_wd[l])
            h = modulate(rmsnorm(x, mix_norm[l]), sh2, sc2)
            y = token_mixing(h, w_in[l], swa_q_norm[l], swa_k_norm[l], swa_sink[l],
                             mla_q_lora_norm[l], mla_w_uq[l], mla_kv_lora_norm[l], mla_w_ukv[l],
                             mla_q_norm[l], mla_k_norm[l], w_out[l])
            x = x + g2[:, None, :] * y
            h = modulate(rmsnorm(x, ffn2_norm[l]), sh3, sc3)
            x = x + 0.5 * g3[:, None, :] * swiglu(h, ffn2_wg[l], ffn2_wu[l], ffn2_wd[l])
            x = rmsnorm(x, final_norm[l])
        return x

    y_prompt = trunk(x_prompt, c_prompt)
    y_sample = trunk(x_sample, c_sample)
    return (y_prompt, y_sample)


_drawn_inputs = setup_inputs


def setup_inputs(seed=0):
    import zlib

    import numpy as np

    out = dict(_drawn_inputs(seed))
    spreads = {}
    factors = {'ffn1_norm': 6.682,
     'mix_norm': 8.0,
     'swa_q_norm': 8.0,
     'swa_k_norm': 8.0,
     'swa_sink': 8.0,
     'mla_q_lora_norm': 8.0,
     'mla_kv_lora_norm': 8.0,
     'mla_q_norm': 8.0,
     'mla_k_norm': 8.0,
     'ffn2_norm': 7.522,
     'final_norm': 2.823}
    for name, (base, spread) in spreads.items():
        noise = np.random.default_rng([zlib.crc32(name.encode()), seed]).standard_normal(out[name].shape)
        drawn = base * np.exp(spread * noise) if base else spread * noise
        out[name] = __import__('jax').numpy.asarray(drawn.astype(out[name].dtype))
    for name, factor in factors.items():
        out[name] = (out[name] * factor).astype(out[name].dtype)
    return out
```

```python
from contextlib import ExitStack

import concourse.bass as bass
import numpy as np
from concourse import mybir

F32 = mybir.dt.float32
F32R = mybir.dt.float32r
BF16 = mybir.dt.bfloat16
ALU = mybir.AluOpType
ACT = mybir.ActivationFunctionType
AX_X = mybir.AxisListType.X

P = 128
D = 1024
KD = D // P
S_PROMPT, S_SAMPLE = 1024, 512
TOK = S_PROMPT + S_SAMPLE
CH = 512
NCH = TOK // CH
NT = TOK // P
TPC = CH // P
F = 2816
FT = F // P
N_MOD = 9
NJ = N_MOD * KD
EPS = 1e-6
HA, KVA, DA = 8, 2, 64
HB, NOPE, ROPE, VB = 8, 64, 32, 64
QKB = NOPE + ROPE
QL, KVL = 256, 128
W_IN = HA * DA + 2 * KVA * DA + QL + KVL + ROPE
SH1, SC1, G1, SH2, SC2, G2, SH3, SC3, G3 = range(N_MOD)

ROW_G = NJ
ROW_QL = ROW_G + 3 * KD
ROW_KVL = ROW_QL + QL // P
ROW_QN = ROW_KVL + 1
ROW_KN = ROW_QN + 1
ROW_C = ROW_KN + 1
NROW = ROW_C + 2 * KD


def build(nc, io):
    with ExitStack() as ctx:
        def sem(name):
            return ctx.enter_context(nc.semaphore(name))

        def sb(scope, name, shape, dt=F32):
            return scope.enter_context(nc.sbuf_tensor(name, shape, dt))

        PS = ctx.enter_context(nc.psum_tensor("PS", [P, 8, 512], F32))

        ident = sb(ctx, "ident", [P, P])
        ones = sb(ctx, "ones", [P, P])
        eps_col = sb(ctx, "eps_col", [P, 3])
        par = sb(ctx, "par", [P, NROW])
        mod = sb(ctx, "mod", [P, NJ, NCH])
        hscale = sb(ctx, "hscale", [P, 3, KD, NCH])
        hgate = sb(ctx, "hgate", [P, 3, KD, NCH])

        rq_a = sb(ctx, "rq_a", [P, NT * HA])
        rq_b = sb(ctx, "rq_b", [P, NT * HB])
        y_st = sb(ctx, "y_st", [P, 2, 2])

        XT = sb(ctx, "XT", [P, KD, TOK])

        s0 = ExitStack()
        ADA_SLOTS = 6
        ada_w_sb = sb(s0, "ada_w_sb", [P, ADA_SLOTS, KD, CH])
        s0.close()
        sH = ExitStack()
        H_hi = sb(sH, "H_hi", [P, KD, TOK], F32R)
        H_lo = sb(sH, "H_lo", [P, KD, TOK], F32R)
        sW = ExitStack()
        W_hi = sb(sW, "W_hi", [P, 3, KD * P], F32R)
        W_lo = sb(sW, "W_lo", [P, 3, KD * P], F32R)
        raw = sb(sW, "raw", [P, 2, KD * P])
        tmp = sb(sW, "tmp", [P, 2, CH])
        s2 = ExitStack()
        rows = sb(s2, "rows", [P, P])
        silu_c = sb(s2, "silu_c", [P, 2, KD])
        x_in = sb(s2, "x_in", [P, 2, D])
        x_sq = sb(s2, "x_sq", [P, 2, CH])
        rstd = sb(s2, "rstd", [P, CH])
        xn = sb(s2, "xn", [P, 2, CH])
        s2.close()
        s3 = ExitStack()
        hid_hi = sb(s3, "hid_hi", [P, 2, TOK], F32R)
        hid_lo = sb(s3, "hid_lo", [P, 2, TOK], F32R)
        s3.close()
        s4 = ExitStack()
        x_out = sb(s4, "x_out", [P, 2, KD, P])
        y_sb = sb(s4, "y_sb", [P, 2, D])
        y_sq = sb(s4, "y_sq", [P, D])
        fgain = sb(s4, "fgain", [P, D])
        s4.close()
        sW.close()
        sA = ExitStack()
        mask = sb(sA, "mask", [P, NT, 2, P], BF16)
        mask3 = sb(sA, "mask3", [P, 3, P])
        ident16 = sb(sA, "ident16", [P, P], BF16)
        sink = sb(sA, "sink", [P, HA])
        sa = sb(sA, "sa", [P, 4, 16])
        kk = sb(sA, "kk", [P, 2, 2 * S_PROMPT])
        vv = sb(sA, "vv", [P, 2, S_PROMPT])
        qa = sb(sA, "qa", [P, 4, P])
        qb = sb(sA, "qb", [P, 2, 2, P])
        probs = sb(sA, "probs", [P, 2, S_PROMPT])
        pT = sb(sA, "pT", [P, 2, S_PROMPT])
        o_sb = sb(sA, "o_sb", [P, 2, P])
        sA.close()
        sH.close()
        sM = ExitStack()
        win_hi = sb(sM, "win_hi", [P, KD, W_IN], F32R)
        win_lo = sb(sM, "win_lo", [P, KD, W_IN], F32R)
        uq_hi = sb(sM, "uq_hi", [P, 2, HB * QKB], F32R)
        uq_lo = sb(sM, "uq_lo", [P, 2, HB * QKB], F32R)
        ukv_hi = sb(sM, "ukv_hi", [P, HB * (NOPE + VB)], F32R)
        ukv_lo = sb(sM, "ukv_lo", [P, HB * (NOPE + VB)], F32R)
        zeros = sb(sM, "zeros", [P, 2 * P])
        xs = sb(sM, "xs", [P, KD, P])
        rt = sb(sM, "rt", [P, P])
        hn = sb(sM, "hn", [P, KD, P])
        ht_hi = sb(sM, "ht_hi", [P, KD, P], F32R)
        ht_lo = sb(sM, "ht_lo", [P, KD, P], F32R)
        z_sb = sb(sM, "z_sb", [P, W_IN])
        z_sq = sb(sM, "z_sq", [P, 640 + QL + KVL + ROPE])
        st = sb(sM, "st", [P, 32])
        krs = sb(sM, "krs", [P, NT])
        krr = sb(sM, "krr", [P, NT, ROPE])
        kr_t = sb(sM, "kr_t", [P, ROPE])
        kr_r = sb(sM, "kr_r", [P, ROPE])
        cT_hi = sb(sM, "cT_hi", [P, 3, P], F32R)
        cT_lo = sb(sM, "cT_lo", [P, 3, P], F32R)
        sw_qk = sb(sM, "sw_qk", [P, 6 * P])
        sw_st = sb(sM, "sw_st", [P, 6 * P])
        qb_sb = sb(sM, "qb_sb", [P, HB, QKB])
        kb_sb = sb(sM, "kb_sb", [P, HB, QKB])
        vb_sb = sb(sM, "vb_sb", [P, HB, VB])
        m_sq = sb(sM, "m_sq", [P, HB, QKB])
        m_t = sb(sM, "m_t", [P, HB, ROPE])
        qT_st = sb(sM, "qT_st", [QKB, HB, P])
        kT_st = sb(sM, "kT_st", [QKB, HB, P])
        rope_in = sb(sM, "rope_in", [P, 2 * DA + 2 * ROPE])
        ropeb_in = sb(sM, "ropeb_in", [P, 2 * ROPE])
        gw_a = sb(sM, "gw_a", [P, 2, 2, DA])
        gw_b = sb(sM, "gw_b", [P, 2, 2, ROPE])
        tab_a = sb(sM, "tab_a", [P, 2, 2, DA])
        tab_bk = sb(sM, "tab_bk", [P, 2, ROPE])
        tab_bq = sb(sM, "tab_bq", [P, 2, ROPE])
        sM.close()

        scr_qa = nc.dram_tensor("scr_qa", (NT, P, 4 * P), F32, kind="Internal").ap()
        scr_ka = nc.dram_tensor("scr_ka", (NT + 2, P, 2 * P), F32, kind="Internal").ap()
        scr_va = nc.dram_tensor("scr_va", (NT + 2, P, KVA * DA), F32, kind="Internal").ap()
        scr_qb = nc.dram_tensor("scr_qb", (NT, QKB, HB, P), F32, kind="Internal").ap()
        scr_kb = nc.dram_tensor("scr_kb", (QKB, HB, TOK), F32, kind="Internal").ap()
        scr_vb = nc.dram_tensor("scr_vb", (NT, P, HB * VB), F32, kind="Internal").ap()

        w_in, w_uq, w_ukv = io["w_in"][0], io["mla_w_uq"][0], io["mla_w_ukv"][0]
        WH = W_IN // 2
        mix_pieces = [(w_in[k * P:(k + 1) * P, i * WH:(i + 1) * WH], WH,
                       win_hi[:, k, i * WH:(i + 1) * WH], win_lo[:, k, i * WH:(i + 1) * WH])
                      for k in range(KD) for i in range(2)]
        mix_pieces += [(w_uq[k * P:(k + 1) * P, :], HB * QKB, uq_hi[:, k, :], uq_lo[:, k, :]) for k in range(2)]
        mix_pieces += [(w_ukv, HB * (NOPE + VB), ukv_hi[:, :], ukv_lo[:, :])]
        N_MW = len(mix_pieces)
        Z_COLS = ((0, 512), (512, 768), (768, W_IN))

        row_plan = [(io["ada_b"].rearrange("a (r m) -> (a r) m", m=P), 0, NJ, P),
                    (io["ffn1_norm"].rearrange("a (r m) -> (a r) m", m=P), ROW_G, KD, P),
                    (io["mix_norm"].rearrange("a (r m) -> (a r) m", m=P), ROW_G + KD, KD, P),
                    (io["ffn2_norm"].rearrange("a (r m) -> (a r) m", m=P), ROW_G + 2 * KD, KD, P),
                    (io["mla_q_lora_norm"].rearrange("a (r m) -> (a r) m", m=P), ROW_QL, QL // P, P),
                    (io["mla_kv_lora_norm"], ROW_KVL, 1, P),
                    (io["mla_q_norm"][:, 0:NOPE], ROW_QN, 1, NOPE),
                    (io["mla_k_norm"][:, 0:NOPE], ROW_KN, 1, NOPE),
                    (io["c_prompt"].rearrange("a (r m) -> (a r) m", m=P), ROW_C, KD, P),
                    (io["c_sample"].rearrange("a (r m) -> (a r) m", m=P), ROW_C + KD, KD, P)]

        rows_landed = sem("rows_landed")
        consts_landed = sem("consts_landed")
        consts_set = sem("consts_set")
        par_psum = sem("par_psum")
        par_ready = sem("par_ready")
        silu_ready = sem("silu_ready")
        x_landed = [sem(f"x_landed{i}") for i in range(2)]
        x_turned = sem("x_turned")
        x_kept_v = sem("x_kept_v")
        x_kept_s = sem("x_kept_s")
        ada_landed = [sem(f"ada_landed{i}") for i in range(ADA_SLOTS)]
        ada_used = sem("ada_used")
        mod_copied = sem("mod_copied")
        mod_ready = sem("mod_ready")
        sq_ready = sem("sq_ready")
        sq_used = sem("sq_used")
        root_ready = sem("root_ready")
        rstd_ready = sem("rstd_ready")
        xn_ready = sem("xn_ready")
        hi_ready = sem("hi_ready")
        h_ready = sem("h_ready")
        raw_landed = [sem(f"raw_landed{i}") for i in range(2)]
        w_hi_ready = sem("w_hi_ready")
        w_ready = sem("w_ready")
        ffn_steps = sem("ffn_steps")
        silu_done = sem("silu_done")
        prod_done = sem("prod_done")
        hid_hi_done = sem("hid_hi_done")
        hid_ready = sem("hid_ready")
        acc_done = sem("acc_done")
        ffn_done = sem("ffn_done")
        out_done = sem("out_done")

        class Steps:
            made = []

            def __init__(self, owner, name, *steps):
                self.sem, self.steps, self.owner, self.i = sem(name), steps, owner, 0
                Steps.made.append(self)

            def at(self, tile, step):
                return tile * len(self.steps) + (4 * len(self.steps) + self.steps.index(step) + 1)

            def tick(self, step):
                assert self.steps[self.i % len(self.steps)] == step, (step, self.i)
                self.i += 1
                return self.sem, 1

        def start_counts(eng, owner):
            for s in Steps.made:
                if s.owner == owner:
                    eng.sem_inc(s.sem, 4 * len(s.steps))

        pN = Steps("pe", "pe_norm", "sum")
        pL = Steps("pe", "pe_latent", "latent_T")
        pZ = Steps("pe", "pe_proj", "z")
        pT_ = Steps("pe", "pe_mla_T", "qT", "kT")
        pS = Steps("pe", "pe_swa_T", "swT")
        pM = Steps("pe", "pe_mla_up", "q", "kv")
        aN = Steps("act", "act_norm", "square", "root", "h_hi")
        aZ = Steps("act", "act_proj", "z_copied", "squares", "c_root", "qk_root", "kr_kept")
        aL = Steps("act", "act_latent", "cT_hi")
        aM = Steps("act", "act_mla", "q_copied", "v_copied", "k_square", "q_root", "k_root")
        aT = Steps("act", "act_mla_T", "qT")
        aS = Steps("act", "act_swa_T", "swT")
        vN = Steps("dve", "dve_norm", "rstd", "xr", "xrs", "h")
        vZ = Steps("dve", "dve_proj", "c_rstd", "ckv", "sums", "qk_rstd", "k_normed", "rot2", "rot1", "k_dup")
        vL = Steps("dve", "dve_latent", "cT_lo")
        vM = Steps("dve", "dve_mla", "q_sum", "rot2", "rot1", "q_rope", "q_rstd", "k_red", "k_sum", "k_rstd", "k_rope")
        vT = Steps("dve", "dve_mla_T", "kT")
        gN = Steps("pool", "pool_norm", "h_lo")
        gZ = Steps("pool", "pool_proj", "tables", "kr1", "kr2")
        gM = Steps("pool", "pool_mla", "table")
        pSc = Steps("pe", "scores_done", "scores")
        pPr = Steps("pe", "probs_turned", "pT")
        pOu = Steps("pe", "outputs_done", "out")
        pX = Steps("pe", "outputs_turned", "oT")
        aE = Steps("act", "exps_done", "exp")
        aP = Steps("act", "pT_copied_act", "pT")
        aX = Steps("act", "oT_hi_done", "o_hi")
        vB = Steps("dve", "bias_done", "bias")
        vR = Steps("dve", "recip_done", "recip")
        vP = Steps("dve", "pT_copied_dve", "pT")
        vO = Steps("dve", "outputs_scaled", "o")
        vX = Steps("dve", "oT_lo_done", "o_lo")
        swa_chain, mla_chain, den_chain = sem("swa_chain"), sem("mla_chain"), sem("den_chain")
        mw_landed = [sem(f"mw_landed{i}") for i in range(2)]
        mw_hi_ready, mw_ready = sem("mw_hi_ready"), sem("mw_ready")
        rope_landed, ropeb_landed, gains_landed = sem("rope_landed"), sem("ropeb_landed"), sem("gains_landed")
        zeros_ready, pads_written = sem("zeros_ready"), sem("pads_written")
        va_written, sw_written, vb_written = sem("va_written"), sem("sw_written"), sem("vb_written")
        mq_written, mk_written = sem("mq_written"), sem("mk_written")
        mask_ready = sem("mask_ready")
        att_consts, k_landed, v_landed = sem("att_consts"), sem("k_landed"), sem("v_landed")
        window_k_landed = [sem(f"window_k_landed{i}") for i in range(2)]
        window_v_landed = [sem(f"window_v_landed{i}") for i in range(2)]
        qa_landed = [sem(f"qa_landed{i}") for i in range(4)]
        qb_landed = [sem(f"qb_landed{i}") for i in range(2)]
        wo_landed = [sem(f"wo_landed{i}") for i in range(2)]
        wo_hi, wo_ready, wo_done, wo_added = sem("wo_hi"), sem("wo_ready"), sem("wo_done"), sem("wo_added")
        x_staged, y_turned, y_scaled, y_summed = sem("x_staged"), sem("y_turned"), sem("y_scaled"), sem("y_summed")
        y_root, y_rstd, fgain_landed = sem("y_root"), sem("y_rstd"), sem("fgain_landed")
        y_written = [sem(f"y_written{i}") for i in range(2)]

        block = ctx.enter_context(nc.Block())

        RS, WS, DS = 2, 3, 2
        NPAIR = FT // 2
        UNITS = 6
        PER_FFN = NPAIR * UNITS

        STEPS = NCH * 4 + NCH * KD

        def gu_step(f, it, n, c):
            return it * STEPS + (f * NPAIR * STEPS + STEPS + n * NCH + c + 1)

        def down_step(f, it, i):
            return it * STEPS + (f * NPAIR * STEPS + STEPS + 4 * NCH + i + 1)

        def pair_start(f, it):
            return it * STEPS + (f * NPAIR * STEPS + STEPS)

        def ffn_loads(sp, f):
            wg, wu, wd = (io[f"ffn{f + 1}_{w}"][0] for w in ("wg", "wu", "wd"))
            wg = wg.rearrange("(k p) f -> p k f", p=P)
            wu = wu.rearrange("(k p) f -> p k f", p=P)
            with sp.Fori(0, NPAIR) as it:
                for n in range(UNITS):
                    sp.wait_ge(w_ready, it * UNITS + (f * PER_FFN + n + 1))
                    if n < 4:
                        src = (wg, wu)[n % 2][:, :, bass.ds((it * 2 + n // 2) * P, P)]
                        dst = raw[:, n % RS, :].rearrange("p (k m) -> p k m", k=KD)
                    else:
                        src = wd[bass.ds((it * 2 + n - 4) * P, P), :]
                        dst = raw[:, n % RS, :]
                    sp.dma_start(dst, src).then_inc(raw_landed[n % RS], 16)

        def ffn_split_hi(act, f, it, n):
            act.wait_ge(raw_landed[n % RS], (it * (UNITS // RS) + (f * PER_FFN + n - n % RS) // RS + 1) * 16)
            act.wait_ge(ffn_steps, pair_start(f, it - 1) + 4 * NCH if n == 0 else
                        pair_start(f, it) + (0, 0, 0, NCH, 2 * NCH, 3 * NCH)[n])
            act.activation(W_hi[:, n % WS, :], raw[:, n % RS, :], ACT.Copy).then_inc(w_hi_ready, 1)

        def ffn_split_lo(pool, f):
            base = f * PER_FFN
            with pool.Fori(0, NPAIR) as it:
                for n in range(UNITS):
                    pool.wait_ge(w_hi_ready, it * UNITS + (base + n + 1))
                    pool.tensor_tensor(W_lo[:, n % WS, :], raw[:, n % RS, :], W_hi[:, n % WS, :].bitcast(F32),
                                       ALU.subtract).then_inc(w_ready, 1)

        def three_pass(pe, out, w_hi, w_lo, m_hi, m_lo, first, last):
            pe.matmul(out, w_hi, m_hi, start=first, stop=False)
            pe.matmul(out, w_hi, m_lo, start=False, stop=False)
            return pe.matmul(out, w_lo, m_hi, start=False, stop=last)

        def ffn_pe(pe, f):
            with pe.Fori(0, NPAIR) as it:
                for n in range(4):
                    t, role = n // 2, n % 2
                    pe.wait_ge(w_ready, it * UNITS + (f * PER_FFN + n + 1 + RS))
                    for c in range(NCH):
                        if n == 0:
                            pe.wait_ge(h_ready, (f * NCH + c + 2) * KD)
                        pe.wait_ge((silu_done, prod_done)[role], it * 6 + (f * FT * NCH + t * NCH + c + 1))
                        for k in range(KD):
                            col = slice(c * CH, (c + 1) * CH)
                            w = slice(k * P, (k + 1) * P)
                            mm = three_pass(pe, PS[:, 3 * role + c, :], W_hi[:, n % WS, w], W_lo[:, n % WS, w],
                                            H_hi[:, k, col], H_lo[:, k, col], k == 0, k == KD - 1)
                        mm.then_inc(ffn_steps, 1)
                for t in range(2):
                    pe.wait_ge(w_ready, it * UNITS + (f * PER_FFN + 5 + t + RS))
                for c in range(NCH):
                    pe.wait_ge(hid_ready, it * 6 + (f * FT * NCH + NCH + c + 1 + 2))
                    for m in range(KD):
                        i = c * KD + m
                        pe.wait_ge(acc_done, it * (NCH * KD) + (f * NPAIR * NCH * KD + i + 1))
                        for t in range(2):
                            w = slice(m * P, (m + 1) * P)
                            col = slice(c * CH, (c + 1) * CH)
                            mm = three_pass(pe, PS[:, 6 + i % DS, :], W_hi[:, 1 + t, w], W_lo[:, 1 + t, w],
                                            hid_hi[:, t, col], hid_lo[:, t, col], t == 0, t == 1)
                        mm.then_inc(ffn_steps, 1)

        def ffn_act(act, f):
            with act.Fori(0, NPAIR) as it:
                for n in range(4):
                    ffn_split_hi(act, f, it, n)
                for t in range(2):
                    for c in range(NCH + 1):
                        if c < NCH:
                            i = t * NCH + c
                            act.wait_ge(ffn_steps, gu_step(f, it, 2 * t, c))
                            act.wait_ge(hid_ready, it * 6 + (f * FT * NCH + i + 1))
                            act.activation(tmp[:, i % 2, :], PS[:, c, :], ACT.Silu).then_inc(silu_done, 1)
                        if c > 0:
                            i = t * NCH + c - 1
                            act.wait_ge(prod_done, it * 6 + (f * FT * NCH + i + 1 + 3))
                            if i == 0:
                                act.wait_ge(ffn_steps, pair_start(f, it))
                            act.activation(hid_hi[:, t, (c - 1) * CH:c * CH], tmp[:, i % 2, :],
                                           ACT.Copy).then_inc(hid_hi_done, 1)
                    if t == 0:
                        ffn_split_hi(act, f, it, 4)
                        ffn_split_hi(act, f, it, 5)

        def ffn_dve(dve, f):
            g = 2 * f
            with dve.Fori(0, NPAIR) as it:
                for t in range(2):
                    for c in range(NCH):
                        i = t * NCH + c
                        dve.wait_ge(silu_done, it * 6 + (f * FT * NCH + i + 1 + 3))
                        dve.wait_ge(ffn_steps, gu_step(f, it, 2 * t + 1, c))
                        dve.tensor_tensor(tmp[:, i % 2, :], tmp[:, i % 2, :], PS[:, 3 + c, :],
                                          ALU.mult).then_inc(prod_done, 1)
                        dve.wait_ge(hid_hi_done, it * 6 + (f * FT * NCH + i + 1))
                        col = slice(c * CH, (c + 1) * CH)
                        dve.tensor_tensor(hid_lo[:, t, col], tmp[:, i % 2, :], hid_hi[:, t, col].bitcast(F32),
                                          ALU.subtract).then_inc(hid_ready, 1)
                for i in range(NCH * KD):
                    c, m = i // KD, i % KD
                    dve.wait_ge(ffn_steps, down_step(f, it, i))
                    xt = XT[:, m, c * CH:(c + 1) * CH]
                    dve.scalar_tensor_tensor(out=xt, in0=PS[:, 6 + i % DS, :], scalar=hgate[:, g, m, c:c + 1], in1=xt,
                                             op0=ALU.mult, op1=ALU.add).then_inc(acc_done, 1)

        def norm_act(act, f):
            n = f * NCH
            with act.Fori(0, NCH) as c:
                col = bass.ds(c * CH, CH)
                for k in range(KD):
                    act.wait_ge(sq_used, (c + n) * KD + (k + 1))
                    act.activation(x_sq[:, k % 2, :], XT[:, k, col], ACT.Square).then_inc(sq_ready, 1)
                act.wait_ge(sq_used, (c + n) * KD + (KD + 2))
                act.wait_ge(h_ready, (c + n + 1) * KD)
                act.activation(rstd[:, :], PS[:, 6, :], ACT.Sqrt, bias=eps_col[:, 0:1],
                               scale=1.0 / D).then_inc(root_ready, 1)
                for k in range(KD):
                    act.wait_ge(xn_ready, (c + n) * KD + (k + 1))
                    act.activation(H_hi[:, k, col], xn[:, k % 2, :], ACT.Identity,
                                   bias=mod[:, (SH1, SH3)[f] * KD + k, bass.ds(c, 1)]).then_inc(hi_ready, 1)

        def norm_pe(pe, f):
            n = f * NCH
            with pe.Fori(0, NCH) as c:
                pe.wait_ge(root_ready, c + (n + 1))
                for k in range(KD):
                    pe.wait_ge(sq_ready, (c + n) * KD + (k + 1))
                    pe.matmul(PS[:, 6, :], ones[:, :], x_sq[:, k % 2, :], start=(k == 0),
                              stop=(k == KD - 1)).then_inc(sq_used, 1)

        def norm_dve(dve, f):
            n = f * NCH
            with dve.Fori(0, NCH) as c:
                col = bass.ds(c * CH, CH)
                dve.wait_ge(root_ready, c + (n + 2))
                dve.reciprocal(rstd[:, :], rstd[:, :]).then_inc(rstd_ready, 1)
                dve.wait_ge(rstd_ready, c + (n + 1))
                for k in range(KD + 1):
                    if k < KD:
                        dve.wait_ge(h_ready, (c + n + 1) * KD + max(k - 1, 0))
                        dve.scalar_tensor_tensor(out=xn[:, k % 2, :], in0=XT[:, k, col],
                                                 scalar=hscale[:, 2 * f, k, bass.ds(c, 1)], in1=rstd[:, :],
                                                 op0=ALU.mult, op1=ALU.mult).then_inc(xn_ready, 1)
                    if k > 0:
                        j = k - 1
                        dve.wait_ge(hi_ready, (c + n) * KD + (j + 1))
                        dve.scalar_tensor_tensor(out=H_lo[:, j, col], in0=xn[:, j % 2, :],
                                                 scalar=mod[:, (SH1, SH3)[f] * KD + j, bass.ds(c, 1)],
                                                 in1=H_hi[:, j, col].bitcast(F32),
                                                 op0=ALU.add, op1=ALU.subtract).then_inc(h_ready, 1)

        ADA_G = NJ * P // CH
        ada_src = io["ada_w"][0].rearrange("(k p) n -> p k n", p=P)

        def start_loads(sp):
            sp.wait_ge(consts_set, 1)
            for src, r0, nr, w in row_plan:
                sp.dma_start(rows[r0:r0 + nr, 0:w], src).then_inc(rows_landed, 16)
            sp.dma_start(ident[:, :], io["ident"]).then_inc(consts_landed, 16)
            for x, first, tiles in ((io["x_prompt"], 0, S_PROMPT // P), (io["x_sample"], S_PROMPT // P, S_SAMPLE // P)):
                with sp.Fori(0, tiles // 2) as it:
                    for i in range(2):
                        sp.wait_ge(x_turned, it * 2 + (first + i + 1))
                        sp.dma_start(x_in[:, i, :], x[0, bass.ds((it * 2 + i) * P, P), :]).then_inc(x_landed[i], 16)
            with sp.Fori(0, ADA_G // ADA_SLOTS) as it:
                for i in range(ADA_SLOTS):
                    sp.wait_ge(ada_used, it * ADA_SLOTS + (i + 1))
                    sp.dma_start(ada_w_sb[:, i, :, :], ada_src[:, :, bass.ds((it * ADA_SLOTS + i) * CH, CH)]) \
                      .then_inc(ada_landed[i], 16)

        def start_pe(pe):
            pe.sem_inc(x_turned, 2)
            pe.sem_inc(ada_used, ADA_SLOTS)
            pe.sem_inc(sq_used, 2)
            pe.sem_inc(ffn_steps, STEPS)
            pe.wait_ge(rows_landed, 16 * len(row_plan))
            pe.wait_ge(consts_landed, 16)
            pe.transpose(PS[:, 4, 0:NROW], rows[0:NROW, :], ident[0:NROW, 0:NROW]).then_inc(par_psum, 1)
            with pe.Fori(0, NT // 2) as it:
                for i in range(2):
                    pe.wait_ge(x_landed[i], (it + 1) * 16)
                    pe.wait_ge(x_kept_v, it * 2 + (i + 1))
                    pe.wait_ge(x_kept_s, it * 2 + (i + 1))
                    for k in range(KD):
                        mm = pe.transpose(PS[:, 2 * i + k // 4, (k % 4) * P:(k % 4 + 1) * P],
                                          x_in[:, i, k * P:(k + 1) * P], ident[:, :])
                    mm.then_inc(x_turned, 1)
            pe.wait_ge(silu_ready, 1)
            with pe.Fori(0, ADA_G // ADA_SLOTS) as it:
                for i in range(ADA_SLOTS):
                    pe.wait_ge(ada_landed[i], (it + 1) * 16)
                    for j in range(CH // P):
                        for k in range(KD):
                            mm = pe.matmul(PS[:, 5, bass.ds((it * ADA_SLOTS + i) * (2 * CH // P) + 2 * j, 2)],
                                           ada_w_sb[:, i, k, j * P:(j + 1) * P], silu_c[:, :, k],
                                           start=(k == 0), stop=(k == KD - 1))
                    mm.then_inc(ada_used, 1)

        def start_act(act):
            act.sem_inc(x_kept_s, 2)
            act.sem_inc(silu_done, 3)
            act.sem_inc(root_ready, 1)
            act.wait_ge(par_psum, 1)
            act.activation(silu_c[:, :, :], PS[:, 4, ROW_C:ROW_C + 2 * KD].rearrange("p (s k) -> p s k", s=2),
                           ACT.Silu).then_inc(silu_ready, 1)
            with act.Fori(0, NT // 2) as it:
                for i in range(2):
                    act.wait_ge(x_turned, it * 2 + (i + 3))
                    act.activation(XT[:, 4:8, bass.ds((it * 2 + i) * P, P)],
                                   PS[:, 2 * i + 1, :].rearrange("p (k m) -> p k m", k=4), ACT.Copy) \
                       .then_inc(x_kept_s, 1)
            act.wait_ge(mod_ready, 1)

        def start_dve(dve):
            dve.sem_inc(x_kept_v, 2)
            dve.sem_inc(prod_done, 3)
            dve.sem_inc(h_ready, KD)
            dve.sem_inc(hid_ready, 2)
            dve.sem_inc(acc_done, 2)
            dve.memset(ones[:, :], 1.0)
            for i, n in enumerate((1, DA, QKB)):
                dve.memset(eps_col[:, i:i + 1], EPS * n)
            dve.memset(rows[:, :], 1.0).then_inc(consts_set, 1)
            dve.wait_ge(silu_ready, 1)
            dve.tensor_copy(par[:, :], PS[:, 4, 0:NROW]).then_inc(par_ready, 1)
            with dve.Fori(0, NT // 2) as it:
                for i in range(2):
                    dve.wait_ge(x_turned, it * 2 + (i + 3))
                    dve.tensor_copy(XT[:, 0:4, bass.ds((it * 2 + i) * P, P)],
                                    PS[:, 2 * i, :].rearrange("p (k m) -> p k m", k=4)).then_inc(x_kept_v, 1)
            dve.wait_ge(par_ready, 1)
            dve.wait_ge(ada_used, ADA_SLOTS + ADA_G)
            out = PS[:, 5, 0:2 * NJ].rearrange("p (j s) -> p j s", s=2)
            for c in range(NCH):
                dve.tensor_tensor(mod[:, :, c], out[:, :, int(c * CH >= S_PROMPT)], par[:, 0:NJ],
                                  ALU.add).then_inc(mod_copied, 1)
            dve.wait_ge(mod_copied, NCH)
            for b in range(3):
                for c in range(NCH):
                    sc, g = (SC1, SC2, SC3)[b] * KD, (G1, G2, G3)[b] * KD
                    dve.scalar_tensor_tensor(out=hscale[:, b, :, c], in0=mod[:, sc:sc + KD, c], scalar=1.0,
                                             in1=par[:, ROW_G + b * KD:ROW_G + (b + 1) * KD],
                                             op0=ALU.add, op1=ALU.mult)
                    mm = dve.tensor_scalar(hgate[:, b, :, c], mod[:, g:g + KD, c], (0.5, 1.0, 0.5)[b], None, ALU.mult)
            mm.then_inc(mod_ready, 1)
            dve.wait_ge(mod_ready, 1)

        WP = W_IN // 2

        def mix_weight_loads(sp):
            sp.wait_ge(w_ready, PER_FFN + RS)
            for i in range(N_MW):
                if i >= RS:
                    sp.wait_ge(mw_ready, i - RS + 1)
                src, n = mix_pieces[i][0], mix_pieces[i][1]
                sp.dma_start(raw[:, i % RS, 0:n], src).then_inc(mw_landed[i % RS], 16)

        def mix_weight_hi(act):
            act.wait_ge(ffn_steps, gu_step(0, NPAIR - 1, 3, NCH - 1))
            for i in range(N_MW):
                _, n, hi, lo = mix_pieces[i]
                act.wait_ge(mw_landed[i % RS], 16 * (i // RS + 1))
                act.activation(hi, raw[:, i % RS, 0:n], ACT.Copy).then_inc(mw_hi_ready, 1)

        def mix_weight_lo(pool):
            for i in range(N_MW):
                _, n, hi, lo = mix_pieces[i]
                pool.wait_ge(mw_hi_ready, i + 1)
                pool.tensor_tensor(lo, raw[:, i % RS, 0:n], hi.bitcast(F32), ALU.subtract).then_inc(mw_ready, 1)

        def tok(u):
            return bass.ds(u * P, P)

        def chunk_of(u):
            return bass.ds(u // TPC, 1)

        def pe_z(pe, u, half):
            if half == 0:
                pe.wait_ge(gN.sem, gN.at(u, "h_lo"))
                pe.wait_ge(aZ.sem, aZ.at(u - 1, "z_copied"))
            for k in range(half * KD // 2, (half + 1) * KD // 2):
                for b, (n0, n1) in enumerate(Z_COLS):
                    mm = three_pass(pe, PS[:, b, 0:n1 - n0], ht_hi[:, k, :], ht_lo[:, k, :],
                                    win_hi[:, k, n0:n1], win_lo[:, k, n0:n1], k == 0, k == KD - 1)
            if half == 1:
                mm.then_inc(*pZ.tick("z"))

        def pe_latent(pe, u):
            pe.wait_ge(vZ.sem, vZ.at(u, "ckv"))
            pe.wait_ge(aN.sem, aN.at(min(u + 1, NT - 1) if isinstance(u, int) else u + 1, "root"))
            for j in range(3):
                c0 = 768 + j * P
                mm = pe.transpose(PS[:, 3, j * P:(j + 1) * P], z_sb[:, c0:c0 + P], ident[:, :])
            mm.then_inc(*pL.tick("latent_T"))

        def pe_sum(pe, u):
            pe.wait_ge(aN.sem, aN.at(u, "square"))
            pe.wait_ge(vL.sem, vL.at(u - 2, "cT_lo"))
            for k in range(KD):
                mm = pe.matmul(PS[:, 3, 0:P], ones[:, :], xs[:, k, :], start=(k == 0), stop=(k == KD - 1))
            mm.then_inc(*pN.tick("sum"))

        def pe_t(pe, u):
            pe.wait_ge(vM.sem, vM.at(u, "q_rope"))
            pe.wait_ge(vM.sem, vM.at(u, "k_rope"))
            pe.wait_ge(aM.sem, aM.at(u, "k_root"))
            for h in range(HB):
                mm = pe.transpose(PS[0:QKB, 4 + h // 4, (h % 4) * P:(h % 4 + 1) * P], qb_sb[:, h, :], ident[:, :])
            mm.then_inc(*pT_.tick("qT"))
            for h in range(HB):
                mm = pe.transpose(PS[0:QKB, 6 + h // 4, (h % 4) * P:(h % 4 + 1) * P], kb_sb[:, h, :], ident[:, :])
            mm.then_inc(*pT_.tick("kT"))

        def pe_s(pe, u):
            pe.wait_ge(vZ.sem, vZ.at(u, "k_dup"))
            pe.wait_ge(aT.sem, aT.at(u - 1, "qT"))
            for j in range(6):
                mm = pe.transpose(PS[:, 4 + j // 4, (j % 4) * P:(j % 4 + 1) * P], sw_qk[:, j * P:(j + 1) * P],
                                  ident[:, :])
            mm.then_inc(*pS.tick("swT"))

        def pe_m(pe, u):
            pe.wait_ge(vL.sem, vL.at(u, "cT_lo"))
            pe.wait_ge(vT.sem, vT.at(u - 1, "kT"))
            for b in range(2):
                for k in range(2):
                    mm = three_pass(pe, PS[:, 6 + b, 0:384], cT_hi[:, k, :], cT_lo[:, k, :],
                                    uq_hi[:, k, b * 384:(b + 1) * 384], uq_lo[:, k, b * 384:(b + 1) * 384],
                                    k == 0, k == 1)
            mm.then_inc(*pM.tick("q"))
            pe.wait_ge(aS.sem, aS.at(u, "swT"))
            for b in range(2):
                mm = three_pass(pe, PS[:, 4 + b, :], cT_hi[:, 2, :], cT_lo[:, 2, :],
                                ukv_hi[:, b * 512:(b + 1) * 512], ukv_lo[:, b * 512:(b + 1) * 512], True, True)
            mm.then_inc(*pM.tick("kv"))

        def act_n1(act, u):
            act.wait_ge(pN.sem, pN.at(u - 1, "sum"))
            act.activation(xs[:, :, :], XT[:, :, tok(u)], ACT.Square).then_inc(*aN.tick("square"))

        def act_n2(act, u):
            act.wait_ge(pN.sem, pN.at(u, "sum"))
            act.wait_ge(vN.sem, vN.at(u - 1, "xr"))
            act.activation(rt[:, :], PS[:, 3, 0:P], ACT.Sqrt, bias=eps_col[:, 0:1], scale=1.0 / D) \
               .then_inc(*aN.tick("root"))

        def act_n3(act, u):
            act.wait_ge(vN.sem, vN.at(u, "h"))
            act.wait_ge(pZ.sem, pZ.at(u - 1, "z"))
            act.activation(ht_hi[:, :, :], hn[:, :, :], ACT.Copy).then_inc(*aN.tick("h_hi"))

        def act_z1(act, u):
            act.wait_ge(pZ.sem, pZ.at(u, "z"))
            act.wait_ge(vZ.sem, vZ.at(u - 1, "k_dup"))
            act.wait_ge(gZ.sem, gZ.at(u - 1, "kr2"))
            act.wait_ge(pL.sem, pL.at(u - 1, "latent_T"))
            act.wait_ge(va_written, (u - 1) * 16 + 32)
            for b, (n0, n1) in enumerate(Z_COLS):
                i = act.activation(z_sb[:, n0:n1], PS[:, b, 0:n1 - n0], ACT.Copy)
            i.then_inc(*aZ.tick("z_copied"))

        def act_z2(act, u):
            act.wait_ge(aZ.sem, aZ.at(u, "z_copied"))
            act.activation(z_sq[:, 0:640], z_sb[:, 0:640], ACT.Square)
            act.activation(z_sq[:, 640:896], z_sb[:, 768:1024], ACT.Square, accum_out=st[:, 10:11])
            act.activation(z_sq[:, 896:1024], z_sb[:, 1024:1152], ACT.Square, accum_out=st[:, 11:12])
            act.activation(z_sq[:, 1024:1056], z_sb[:, 1152:1184], ACT.Square, accum_out=krs[:, bass.ds(u, 1)]) \
               .then_inc(*aZ.tick("squares"))
            act.wait_ge(aZ.sem, aZ.at(u, "squares"))
            act.activation(st[:, 10:11], st[:, 10:11], ACT.Sqrt, bias=eps_col[:, 0:1], scale=1.0 / QL)
            act.activation(st[:, 11:12], st[:, 11:12], ACT.Sqrt, bias=eps_col[:, 0:1], scale=1.0 / KVL) \
               .then_inc(*aZ.tick("c_root"))
            act.wait_ge(vZ.sem, vZ.at(u, "sums"))
            act.activation(st[:, 0:8], st[:, 0:8], ACT.Sqrt, bias=eps_col[:, 1:2])
            act.activation(st[:, 8:10], st[:, 8:10], ACT.Sqrt, bias=eps_col[:, 0:1], scale=1.0 / DA) \
               .then_inc(*aZ.tick("qk_root"))
            act.wait_ge(gZ.sem, gZ.at(u, "kr2"))
            act.activation(krr[:, bass.ds(u, 1), :], kr_r[:, :].unsqueeze(1), ACT.Copy).then_inc(*aZ.tick("kr_kept"))

        def act_l(act, u):
            act.wait_ge(pL.sem, pL.at(u, "latent_T"))
            act.wait_ge(pM.sem, pM.at(u - 1, "kv"))
            for j in range(3):
                r = (ROW_QL, ROW_QL + 1, ROW_KVL)[j]
                i = act.activation(cT_hi[:, j, :], PS[:, 3, j * P:(j + 1) * P], ACT.Copy, scale=par[:, r:r + 1])
            i.then_inc(*aL.tick("cT_hi"))

        def act_m(act, u):
            act.wait_ge(pM.sem, pM.at(u, "q"))
            act.wait_ge(pT_.sem, pT_.at(u - 1, "qT"))
            q2 = qb_sb[:, :, :].rearrange("p (b h) d -> p b (h d)", b=2)
            s2_ = m_sq[:, :, :].rearrange("p (b h) d -> p b (h d)", b=2)
            act.activation(q2, PS[:, 6:8, 0:384], ACT.Copy)
            act.activation(s2_, PS[:, 6:8, 0:384], ACT.Square).then_inc(*aM.tick("q_copied"))
            act.wait_ge(pM.sem, pM.at(u, "kv"))
            act.wait_ge(vb_written, (u - 1) * 16 + 32)
            kv = PS[:, 4:6, :].rearrange("p b (h c) -> p (b h) c", c=NOPE + VB)
            act.activation(vb_sb[:, :, :], kv[:, :, NOPE:NOPE + VB], ACT.Copy).then_inc(*aM.tick("v_copied"))
            act.wait_ge(vM.sem, vM.at(u, "q_sum"))
            act.activation(m_sq[:, :, 0:NOPE], kv[:, :, 0:NOPE], ACT.Square).then_inc(*aM.tick("k_square"))
            act.activation(st[:, 16:24], st[:, 16:24], ACT.Sqrt, bias=eps_col[:, 2:3]).then_inc(*aM.tick("q_root"))
            act.wait_ge(vM.sem, vM.at(u, "k_sum"))
            act.activation(st[:, 24:32], st[:, 24:32], ACT.Sqrt, bias=eps_col[:, 0:1], scale=1.0 / QKB) \
               .then_inc(*aM.tick("k_root"))

        def act_t(act, u):
            act.wait_ge(pT_.sem, pT_.at(u, "qT"))
            act.wait_ge(mq_written, (u - 1) * 16 + 32)
            act.activation(qT_st[:, :, :].rearrange("p (b h) t -> p b (h t)", b=2), PS[0:QKB, 4:6, :], ACT.Copy,
                           scale=par[0:QKB, ROW_QN:ROW_QN + 1]).then_inc(*aT.tick("qT"))

        def act_s(act, u):
            act.wait_ge(pS.sem, pS.at(u, "swT"))
            act.wait_ge(sw_written, (u - 1) * 32 + 64)
            act.activation(sw_st[:, 0:4 * P], PS[:, 4, :], ACT.Copy)
            act.activation(sw_st[:, 4 * P:6 * P], PS[:, 5, 0:2 * P], ACT.Copy).then_inc(*aS.tick("swT"))

        def dve_n1(dve, u):
            dve.wait_ge(aN.sem, aN.at(u, "root"))
            dve.reciprocal(rt[:, :], rt[:, :]).then_inc(*vN.tick("rstd"))
            dve.wait_ge(vN.sem, vN.at(u, "rstd"))
            dve.wait_ge(aN.sem, aN.at(u - 1, "h_hi"))
            dve.wait_ge(gN.sem, gN.at(u - 1, "h_lo"))
            dve.tensor_tensor(hn[:, :, :], XT[:, :, tok(u)], rt[:, None, :].to_broadcast([P, KD, P]), ALU.mult) \
               .then_inc(*vN.tick("xr"))
            dve.wait_ge(vN.sem, vN.at(u, "xr"))
            dve.tensor_tensor(hn[:, :, :], hn[:, :, :], hscale[:, 1, :, chunk_of(u)].to_broadcast([P, KD, P]), ALU.mult) \
               .then_inc(*vN.tick("xrs"))
            dve.wait_ge(vN.sem, vN.at(u, "xrs"))
            dve.tensor_tensor(hn[:, :, :], hn[:, :, :], mod[:, SH2 * KD:(SH2 + 1) * KD, chunk_of(u)].to_broadcast([P, KD, P]),
                              ALU.add).then_inc(*vN.tick("h"))

        def dve_z(dve, u):
            dve.wait_ge(aZ.sem, aZ.at(u, "c_root"))
            dve.reciprocal(st[:, 10:12], st[:, 10:12]).then_inc(*vZ.tick("c_rstd"))
            dve.wait_ge(vZ.sem, vZ.at(u, "c_rstd"))
            dve.tensor_scalar(z_sb[:, 768:1024], z_sb[:, 768:1024], st[:, 10:11], None, ALU.mult)
            dve.tensor_scalar(z_sb[:, 1024:1152], z_sb[:, 1024:1152], st[:, 11:12], None, ALU.mult) \
               .then_inc(*vZ.tick("ckv"))
            dve.tensor_reduce(st[:, 0:10], z_sq[:, 0:640].rearrange("p (h d) -> p h d", d=DA), AX_X, ALU.add) \
               .then_inc(*vZ.tick("sums"))
            zq = z_sb[:, 0:512].rearrange("p (h d) -> p h d", d=DA)
            zk = z_sb[:, 512:640].rearrange("p (h d) -> p h d", d=DA)
            t2 = z_sq[:, 0:640].rearrange("p (h d) -> p h d", d=DA)
            o = sw_qk[:, 0:512].rearrange("p (h d) -> p h d", d=DA)
            dve.wait_ge(aZ.sem, aZ.at(u, "qk_root"))
            dve.reciprocal(rq_a[:, bass.ds(u * HA, HA)], st[:, 0:8])
            dve.reciprocal(st[:, 8:10], st[:, 8:10]).then_inc(*vZ.tick("qk_rstd"))
            dve.wait_ge(vZ.sem, vZ.at(u, "qk_rstd"))
            dve.tensor_tensor(zk, zk, st[:, 8:10, None].to_broadcast([P, 2, DA]), ALU.mult).then_inc(*vZ.tick("k_normed"))
            dve.wait_ge(gZ.sem, gZ.at(u, "tables"))
            dve.wait_ge(vZ.sem, vZ.at(u, "k_normed"))
            hd = DA // 2
            for z, n, s, h0 in ((zq, HA, 0, 0), (zk, KVA, 1, HA)):
                for a in range(2):
                    f = slice(a * hd, (a + 1) * hd)
                    g = slice((1 - a) * hd, (2 - a) * hd)
                    i = dve.tensor_tensor(t2[:, h0:h0 + n, f], z[:, :, g],
                                          tab_a[:, s, 1:2, f].to_broadcast([P, n, hd]), ALU.mult)
            i.then_inc(*vZ.tick("rot2"))
            dve.wait_ge(pS.sem, pS.at(u - 1, "swT"))
            dve.wait_ge(vZ.sem, vZ.at(u, "rot2"))
            dve.tensor_tensor(o, zq, tab_a[:, 0, 0:1, :].to_broadcast([P, HA, DA]), ALU.mult)
            dve.tensor_tensor(zk, zk, tab_a[:, 1, 0:1, :].to_broadcast([P, KVA, DA]), ALU.mult) \
               .then_inc(*vZ.tick("rot1"))
            dve.wait_ge(vZ.sem, vZ.at(u, "rot1"))
            dve.tensor_tensor(o, o, t2[:, 0:HA, :], ALU.add)
            ok = sw_qk[:, 512:768].rearrange("p (g e d) -> p g e d", g=KVA, e=2)
            for e in range(2):
                i = dve.tensor_tensor(ok[:, :, e, :], zk, t2[:, HA:HA + KVA, :], ALU.add)
            i.then_inc(*vZ.tick("k_dup"))

        def dve_l(dve, u):
            dve.wait_ge(aL.sem, aL.at(u, "cT_hi"))
            for j in range(3):
                r = (ROW_QL, ROW_QL + 1, ROW_KVL)[j]
                i = dve.scalar_tensor_tensor(out=cT_lo[:, j, :], in0=PS[:, 3, j * P:(j + 1) * P], scalar=par[:, r:r + 1],
                                             in1=cT_hi[:, j, :].bitcast(F32), op0=ALU.mult, op1=ALU.subtract)
            i.then_inc(*vL.tick("cT_lo"))

        def dve_m(dve, u):
            dve.wait_ge(aM.sem, aM.at(u, "q_copied"))
            dve.tensor_reduce(st[:, 16:24], m_sq[:, :, :], AX_X, ALU.add).then_inc(*vM.tick("q_sum"))
            qr = qb_sb[:, :, NOPE:QKB]
            hd = ROPE // 2
            dve.wait_ge(gM.sem, gM.at(u, "table"))
            for a in range(2):
                f, g = slice(a * hd, (a + 1) * hd), slice((1 - a) * hd, (2 - a) * hd)
                i = dve.tensor_tensor(m_t[:, :, f], qr[:, :, g], tab_bq[:, 1:2, f].to_broadcast([P, HB, hd]), ALU.mult)
            i.then_inc(*vM.tick("rot2"))
            dve.wait_ge(vM.sem, vM.at(u, "rot2"))
            dve.tensor_tensor(qr, qr, tab_bq[:, 0:1, :].to_broadcast([P, HB, ROPE]), ALU.mult).then_inc(*vM.tick("rot1"))
            dve.wait_ge(vM.sem, vM.at(u, "rot1"))
            dve.tensor_tensor(qr, qr, m_t[:, :, :], ALU.add).then_inc(*vM.tick("q_rope"))
            dve.wait_ge(aM.sem, aM.at(u, "q_root"))
            dve.reciprocal(rq_b[:, bass.ds(u * HB, HB)], st[:, 16:24]).then_inc(*vM.tick("q_rstd"))
            dve.wait_ge(aM.sem, aM.at(u, "k_square"))
            dve.tensor_reduce(st[:, 24:32], m_sq[:, :, 0:NOPE], AX_X, ALU.add).then_inc(*vM.tick("k_red"))
            dve.wait_ge(vM.sem, vM.at(u, "k_red"))
            dve.tensor_scalar(st[:, 24:32], st[:, 24:32], krs[:, bass.ds(u, 1)], None, ALU.add) \
               .then_inc(*vM.tick("k_sum"))
            dve.wait_ge(aM.sem, aM.at(u, "k_root"))
            dve.reciprocal(st[:, 24:32], st[:, 24:32]).then_inc(*vM.tick("k_rstd"))
            dve.wait_ge(vM.sem, vM.at(u, "k_rstd"))
            dve.wait_ge(aZ.sem, aZ.at(u, "kr_kept"))
            dve.wait_ge(pT_.sem, pT_.at(u - 1, "kT"))
            kv = PS[:, 4:6, :].rearrange("p b (h c) -> p (b h) c", c=NOPE + VB)
            rk = st[:, 24:32].unsqueeze(2)
            dve.tensor_tensor(kb_sb[:, :, 0:NOPE], kv[:, :, 0:NOPE], rk.to_broadcast([P, HB, NOPE]), ALU.mult)
            dve.tensor_tensor(kb_sb[:, :, NOPE:QKB], krr[:, bass.ds(u, 1), :].to_broadcast([P, HB, ROPE]),
                              rk.to_broadcast([P, HB, ROPE]), ALU.mult).then_inc(*vM.tick("k_rope"))

        def dve_t(dve, u):
            dve.wait_ge(pT_.sem, pT_.at(u, "kT"))
            dve.wait_ge(mk_written, (u - 1) * 16 + 32)
            dve.tensor_scalar(kT_st[:, :, :].rearrange("p (b h) t -> p b (h t)", b=2), PS[0:QKB, 6:8, :],
                              par[0:QKB, ROW_KN:ROW_KN + 1], None, ALU.mult).then_inc(*vT.tick("kT"))

        def pool_n(pool, u):
            pool.wait_ge(aN.sem, aN.at(u, "h_hi"))
            pool.tensor_tensor(ht_lo[:, :, :], hn[:, :, :], ht_hi[:, :, :].bitcast(F32), ALU.subtract) \
                .then_inc(*gN.tick("h_lo"))

        def pool_z(pool, u):
            pool.wait_ge(rope_landed, u * 16 + 16)
            pool.wait_ge(vZ.sem, vZ.at(u - 1, "rot1"))
            pool.tensor_tensor(tab_a[:, :, :, :].rearrange("p s v d -> p s (v d)"), gw_a[:, :, :, :].rearrange("p s v d -> p s (v d)"),
                               rope_in[:, 0:2 * DA].unsqueeze(1).to_broadcast([P, 2, 2 * DA]), ALU.mult)
            pool.tensor_tensor(tab_bk[:, :, :].rearrange("p v d -> p (v d)"), gw_b[:, 1, :, :].rearrange("p v d -> p (v d)"),
                               rope_in[:, 2 * DA:], ALU.mult).then_inc(*gZ.tick("tables"))
            pool.wait_ge(gZ.sem, gZ.at(u, "tables"))
            pool.wait_ge(aZ.sem, aZ.at(u, "z_copied"))
            kr = z_sb[:, 1152:1184]
            hd = ROPE // 2
            pool.wait_ge(aZ.sem, aZ.at(u - 1, "kr_kept"))
            pool.tensor_tensor(kr_r[:, :], kr, tab_bk[:, 0, :], ALU.mult)
            for a in range(2):
                f, g = slice(a * hd, (a + 1) * hd), slice((1 - a) * hd, (2 - a) * hd)
                i = pool.tensor_tensor(kr_t[:, f], kr[:, g], tab_bk[:, 1, f], ALU.mult)
            i.then_inc(*gZ.tick("kr1"))
            pool.wait_ge(gZ.sem, gZ.at(u, "kr1"))
            pool.tensor_tensor(kr_r[:, :], kr_r[:, :], kr_t[:, :], ALU.add) \
                .then_inc(*gZ.tick("kr2"))

        def pool_m(pool, u):
            pool.wait_ge(ropeb_landed, u * 16 + 16)
            pool.wait_ge(vM.sem, vM.at(u - 1, "rot1"))
            pool.tensor_tensor(tab_bq[:, :, :].rearrange("p v d -> p (v d)"), gw_b[:, 0, :, :].rearrange("p v d -> p (v d)"),
                               ropeb_in[:, :], ALU.mult).then_inc(*gM.tick("table"))

        def sp_z(sp, u):
            sp.wait_ge(aZ.sem, aZ.at(u, "z_copied"))
            sp.dma_start(scr_va[bass.ds(u + 1, 1)].rearrange("a p c -> p (a c)"), z_sb[:, 640:768]).then_inc(va_written, 16)

        def sp_rope(sp, u):
            sp.wait_ge(gZ.sem, gZ.at(u - 1, "tables"))
            sp.dma_start(rope_in[:, :], io["rope"][bass.ds(u, 1)].rearrange("a p d -> p (a d)")).then_inc(rope_landed, 16)

        def sp_ropeb(sp, u):
            sp.wait_ge(gM.sem, gM.at(u - 1, "table"))
            sp.dma_start(ropeb_in[:, :], io["rope"][bass.ds(u, 1), :, 2 * DA:].rearrange("a p d -> p (a d)")) \
              .then_inc(ropeb_landed, 16)

        def sp_s(sp, u):
            sp.wait_ge(aS.sem, aS.at(u, "swT"))
            sp.dma_start(scr_qa[bass.ds(u, 1)].rearrange("a p c -> p (a c)"), sw_st[:, 0:4 * P]).then_inc(sw_written, 16)
            sp.dma_start(scr_ka[bass.ds(u + 1, 1)].rearrange("a p c -> p (a c)"), sw_st[:, 4 * P:]).then_inc(sw_written, 16)

        def sp_m(sp, u):
            sp.wait_ge(aM.sem, aM.at(u, "v_copied"))
            sp.dma_start(scr_vb[bass.ds(u, 1)].rearrange("a p c -> p (a c)"), vb_sb[:, :, :].rearrange("p h d -> p (h d)")) \
              .then_inc(vb_written, 16)

        def sp_t(sp, u):
            sp.wait_ge(aT.sem, aT.at(u, "qT"))
            sp.dma_start(scr_qb[bass.ds(u, 1)].rearrange("a p h t -> p (a h) t"), qT_st[:, :, :]).then_inc(mq_written, 16)
            sp.wait_ge(vT.sem, vT.at(u, "kT"))
            sp.dma_start(scr_kb[:, :, tok(u)], kT_st[:, :, :]).then_inc(mk_written, 16)

        def turns(eng, plan):
            lags = [lag for _, lag in plan]
            lo, hi = max(lags), NT + min(lags)
            for u in range(min(lags), lo):
                for stage, lag in plan:
                    if 0 <= u - lag < NT:
                        stage(eng, u - lag)
            with eng.Fori(lo, hi) as u:
                for stage, lag in plan:
                    stage(eng, u - lag)
            for u in range(hi, NT + max(lags)):
                for stage, lag in plan:
                    if 0 <= u - lag < NT:
                        stage(eng, u - lag)

        def mix_pe(pe):
            pe.wait_ge(mw_ready, N_MW)
            turns(pe, [(lambda e, u: pe_z(e, u, 0), 0), (pe_latent, 1), (pe_sum, -1), (lambda e, u: pe_z(e, u, 1), 0),
                       (pe_t, 2), (pe_s, 1), (pe_m, 1)])

        def mix_act(act):
            act.wait_ge(acc_done, DS + NPAIR * NCH * KD)
            act.wait_ge(mw_ready, N_MW)
            turns(act, [(act_n1, -1), (act_m, 2), (act_l, 1), (act_n2, -1), (act_n3, -1),
                        (act_t, 2), (act_z1, 0), (act_s, 1), (act_z2, 0)])

        def mix_dve(dve):
            dve.wait_ge(mw_ready, N_MW)
            turns(dve, [(dve_m, 2), (dve_l, 1), (dve_n1, -1), (dve_t, 2), (dve_z, 0)])

        def mix_pool(pool):
            pool.wait_ge(mw_ready, N_MW)
            pool.wait_ge(acc_done, DS + NPAIR * NCH * KD)
            pool.memset(zeros[:, :], 0.0).then_inc(zeros_ready, 1)
            pool.wait_ge(gains_landed, 16 * 12)
            turns(pool, [(pool_m, 2), (pool_n, -1), (pool_z, 0)])

        def write_pads(sp):
            sp.wait_ge(zeros_ready, 1)
            for t in (0, NT + 1):
                sp.dma_start(scr_ka[t], zeros[:, :]).then_inc(pads_written, 16)
                sp.dma_start(scr_va[t], zeros[:, 0:P]).then_inc(pads_written, 16)

        def mix_dma(sp):
            sp.wait_ge(mw_ready, N_MW)
            sp.wait_ge(acc_done, DS + NPAIR * NCH * KD)
            gain = {"a": (DA, ("swa_q_norm", "swa_k_norm"), gw_a, 0), "b": (ROPE, ("mla_q_norm", "mla_k_norm"), gw_b, NOPE)}
            for d, names, dst, c0 in gain.values():
                for s, name in enumerate(names):
                    g, hd = io[name][0, :], d // 2
                    sp.dma_start(dst[:, s, 0, :], g[c0:c0 + d].partition_broadcast(P)).then_inc(gains_landed, 16)
                    sp.dma_start(dst[:, s, 1, 0:hd], g[c0 + hd:c0 + d].partition_broadcast(P)).then_inc(gains_landed, 16)
                    sp.dma_start(dst[:, s, 1, hd:d], g[c0:c0 + hd].partition_broadcast(P)).then_inc(gains_landed, 16)
            write_pads(sp)
            turns(sp, [(sp_rope, 0), (sp_ropeb, 2), (sp_m, 2), (sp_t, 2), (sp_z, 0), (sp_s, 1)])

        def o_col(u):
            return bass.ds(u * P, P)

        class Kind:
            def __init__(self, name, unit0, groups, x0, tile0, nk, q0, kv0):
                self.name, self.unit0, self.groups, self.x0, self.tile0, self.nk = name, unit0, groups, x0, tile0, nk
                self.q0, self.kv0 = q0, kv0

        PAIRS = HB // 2
        swa = Kind("swa", 0, NT // 2, 0, 0, 3, 0, 0)
        mla_p = Kind("mla", 4 * NT, PAIRS * (S_PROMPT // P) // 4, 4 * NT, 0, S_PROMPT // P, 0, 0)
        mla_s = Kind("mla", mla_p.unit0 + 8 * mla_p.groups, PAIRS * (S_SAMPLE // P) // 4,
                     mla_p.x0 + 4 * mla_p.groups, S_PROMPT // P, S_SAMPLE // P, 2 * mla_p.groups, PAIRS)
        kinds = (swa, mla_p, mla_s)
        NV = mla_s.unit0 + 8 * mla_s.groups
        NX = mla_s.x0 + 4 * mla_s.groups

        class Unit:
            def __init__(self, kind, g, k):
                if k < 0:
                    g, k = g - 1, k + 8
                self.kind, self.k, self.par = kind, k, k % 2
                self.v = g * 8 + (kind.unit0 + k)
                if kind is swa:
                    self.j = k % 4
                    self.x = self.v
                    self.tile = g * 2 + k // 4
                    self.kt_out, self.kv_slot = self.j, k // 4
                    self.heads, self.last_of_pair = (2 * self.j, 2 * self.j + 1), True
                    self.kv_no, self.q_no = g, self.tile
                    self.o_slot = k % 2
                else:
                    gpp = kind.nk // 4
                    self.x = g * 4 + (kind.x0 + k // 2)
                    pair = g // gpp
                    self.tile = (g % gpp) * 4 + (kind.tile0 + k // 2)
                    self.kt_out, self.kv_slot = pair + 4, pair % 2
                    self.head, self.last_of_pair = pair * 2 + k % 2, k % 2 == 1
                    self.kv_no, self.q_no = pair + kind.kv0, g * 2 + (kind.q0 + k // 4)
                    self.q_slot = self.o_slot = (k // 2) % 2

        def unit_of(v):
            for kind in reversed(kinds):
                if v >= kind.unit0:
                    return Unit(kind, (v - kind.unit0) // 8, (v - kind.unit0) % 8)

        def attention_turns(eng, plan):
            for kind in kinds:
                for v in range(kind.unit0, kind.unit0 + 8):
                    for stage, lag in plan:
                        if v >= lag:
                            stage(eng, unit_of(v - lag))
                with eng.Fori(1, kind.groups) as g:
                    for k in range(8):
                        for stage, lag in plan:
                            stage(eng, Unit(kind, g, k - lag))
            for v in range(NV, NV + max(lag for _, lag in plan)):
                for stage, lag in plan:
                    if v - lag < NV:
                        stage(eng, unit_of(v - lag))

        def q_loaded(eng, un):
            eng.wait_ge(qa_landed[un.j] if un.kind is swa else qb_landed[un.q_slot], un.q_no * 16 + 16)

        def pe_scores(pe, un):
            b = 2 * un.par
            q_loaded(pe, un)
            pe.wait_ge(window_k_landed[un.kv_slot] if un.kind is swa else k_landed, un.kv_no * 16 + 16)
            pe.wait_ge(aE.sem, aE.at(un.v - 2, "exp"))
            if un.kind is swa:
                for e in range(2):
                    rows_, g = slice(e * DA, (e + 1) * DA), un.j // 2
                    win = kk[rows_, un.kv_slot, 0:3 * 2 * P].rearrange("p (t g c) -> p t g c", t=3, g=2)
                    pe.matmul(PS[:, b + e, 0:3 * P], qa[rows_, un.j, :], win[:, :, g, :], start=True, stop=True)
                    pe.matmul(PS[:, b + e, 0:P], ident16[:, :], mask[:, bass.ds(un.tile, 1), 0, :], start=False,
                              stop=True, skip_group_check=True)
                    mm = pe.matmul(PS[:, b + e, 2 * P:3 * P], ident16[:, :], mask[:, bass.ds(un.tile, 1), 1, :],
                                   start=False, stop=True, skip_group_check=True)
            else:
                for half in range(un.kind.nk // 4):
                    c0 = un.par * un.kind.nk * P + half * CH
                    mm = pe.matmul(PS[:, b + half, :], qb[0:QKB, un.q_slot, un.par, :],
                                   kk[0:QKB, bass.ds(un.kv_slot, 1), c0:c0 + CH], start=True, stop=True)
            mm.then_inc(*pSc.tick("scores"))

        def pe_probs(pe, un):
            pe.wait_ge(aE.sem, aE.at(un.v, "exp"))
            pe.wait_ge(aP.sem, aP.at(un.v - 1, "pT"))
            pe.wait_ge(vP.sem, vP.at(un.v - 1, "pT"))
            n = 6 if un.kind is swa else un.kind.nk
            per = 3 if un.kind is swa else 4 if n == 8 else 2
            for j in range(n):
                mm = pe.transpose(PS[:, 4 + j // per, (j % per) * P:(j % per + 1) * P],
                                  probs[:, un.par, j * P:(j + 1) * P], ident[:, :])
            mm.then_inc(*pPr.tick("pT"))

        def pe_out(pe, un):
            pe.wait_ge(aP.sem, aP.at(un.v, "pT"))
            pe.wait_ge(vP.sem, vP.at(un.v, "pT"))
            pe.wait_ge(window_v_landed[un.kv_slot] if un.kind is swa else v_landed, un.kv_no * 16 + 16)
            bank = PS[:, 6 + un.par, :]
            out_read(pe, un, 2)
            if un.kind is swa:
                g = un.j // 2
                for e in range(2):
                    for t in range(3):
                        mm = pe.matmul(bank[:, e * DA:(e + 1) * DA], pT[:, un.par, (3 * e + t) * P:(3 * e + t + 1) * P],
                                       vv[:, un.kv_slot, t * P + g * DA:t * P + (g + 1) * DA],
                                       start=(t == 0), stop=(t == 2))
            else:
                for t in range(un.kind.nk):
                    mm = pe.matmul(bank[:, 0:VB], pT[:, un.par, t * P:(t + 1) * P],
                                   vv[:, bass.ds(un.kv_slot, 1), t * P + un.par * VB:t * P + (un.par + 1) * VB],
                                   start=(t == 0), stop=(t == un.kind.nk - 1))
            mm.then_inc(*pOu.tick("out"))

        def out_read(eng, un, ago):
            eng.wait_ge(vO.sem, vO.at(un.v - ago, "o"))
            eng.wait_ge(vX.sem, vX.at(un.x - (1 if un.kind is not swa and un.last_of_pair else 2), "o_lo"))

        def pe_turn(pe, un):
            if un.last_of_pair:
                pe.wait_ge(vO.sem, vO.at(un.v, "o"))
                pe.transpose(PS[:, 6 + un.par, P:2 * P], o_sb[:, un.o_slot, :], ident[:, :]).then_inc(*pX.tick("oT"))

        def act_exp(act, un):
            b, s = 2 * un.par, un.k % 4
            act.wait_ge(vB.sem, vB.at(un.v, "bias"))
            act.wait_ge(pPr.sem, pPr.at(un.v - 2, "pT"))
            if un.kind is swa:
                for e in range(2):
                    act.activation(probs[:, un.par, 3 * P * e:3 * P * (e + 1)], PS[:, b + e, 0:3 * P], ACT.Exp,
                                   bias=sa[:, s, 4 + e:5 + e], scale=rq_a[:, bass.ds(un.tile * HA + un.heads[e], 1)],
                                   accum_out=sa[:, s, 8 + e:9 + e])
                act.activation(sa[:, s, 10:12], sa[:, s, 6:8], ACT.Exp).then_inc(*aE.tick("exp"))
            else:
                n = un.kind.nk * P
                act.activation(probs[:, un.par, 0:n], PS[:, b:b + n // CH, :].rearrange("p b c -> p (b c)"), ACT.Exp,
                               bias=sa[:, s, 4:5], scale=rq_b[:, bass.ds(un.tile * HB + un.head, 1)],
                               accum_out=sa[:, s, 8:9]).then_inc(*aE.tick("exp"))

        def pT_half(un, b):
            n = (3 if un.kind is swa else un.kind.nk // 2) * P
            return pT[:, un.par, b * n:(b + 1) * n], PS[:, 4 + b, 0:n]

        def act_pT(act, un):
            act.wait_ge(pPr.sem, pPr.at(un.v, "pT"))
            act.wait_ge(pOu.sem, pOu.at(un.v - 2, "out"))
            dst, src = pT_half(un, 0)
            act.activation(dst, src, ACT.Copy).then_inc(*aP.tick("pT"))

        def act_oT(act, un):
            if un.last_of_pair:
                act.wait_ge(pX.sem, pX.at(un.x, "oT"))
                act.activation(H_hi[:, slice_of(un.kt_out), o_col(un.tile)], PS[:, 6 + un.par, P:2 * P], ACT.Copy) \
                   .then_inc(*aX.tick("o_hi"))

        def slice_of(i):
            return slice(i, i + 1) if isinstance(i, int) else bass.ds(i, 1)

        def dve_max(dve, un):
            b, s = 2 * un.par, un.k % 4
            S_ = sa[:, s, :]
            dve.wait_ge(pSc.sem, pSc.at(un.v, "scores"))
            dve.wait_ge(vR.sem, vR.at(un.v - 4, "recip"))
            if un.kind is swa:
                x = un.v * 3
                dve.tensor_reduce(S_[:, 0:2], PS[:, b:b + 2, 0:3 * P], AX_X, ALU.max).then_inc(swa_chain, 1)
                dve.wait_ge(swa_chain, x + 1)
                dve.tensor_tensor(S_[:, 2:4], S_[:, 0:2], rq_a[:, bass.ds(un.tile * HA + un.heads[0], 2)], ALU.mult) \
                   .then_inc(swa_chain, 1)
                dve.wait_ge(swa_chain, x + 2)
                dve.tensor_tensor(S_[:, 2:4], S_[:, 2:4], sink[:, un.heads[0]:un.heads[0] + 2], ALU.max) \
                   .then_inc(swa_chain, 1)
                dve.wait_ge(swa_chain, x + 3)
                dve.tensor_tensor(S_[:, 6:8], sink[:, un.heads[0]:un.heads[0] + 2], S_[:, 2:4], ALU.subtract)
                dve.tensor_scalar(S_[:, 4:6], S_[:, 2:4], -1.0, None, ALU.mult).then_inc(*vB.tick("bias"))
            else:
                x = un.v - mla_p.unit0
                nb = un.kind.nk // 4
                dve.tensor_reduce(S_[:, 0:1], PS[:, b:b + nb, :].rearrange("p b c -> p (b c)"), AX_X, ALU.max) \
                   .then_inc(mla_chain, 1)
                dve.wait_ge(mla_chain, x + 1)
                dve.tensor_scalar(S_[:, 4:5], S_[:, 0:1], rq_b[:, bass.ds(un.tile * HB + un.head, 1)], -1.0,
                                  ALU.mult, ALU.mult).then_inc(*vB.tick("bias"))

        def dve_recip(dve, un):
            s = un.k % 4
            dve.wait_ge(aE.sem, aE.at(un.v, "exp"))
            if un.kind is swa:
                dve.tensor_tensor(sa[:, s, 12:14], sa[:, s, 8:10], sa[:, s, 10:12], ALU.add).then_inc(den_chain, 1)
                dve.wait_ge(den_chain, un.v + 1)
                dve.reciprocal(sa[:, s, 12:14], sa[:, s, 12:14]).then_inc(*vR.tick("recip"))
            else:
                dve.reciprocal(sa[:, s, 12:13], sa[:, s, 8:9]).then_inc(*vR.tick("recip"))

        def dve_pT(dve, un):
            dve.wait_ge(pPr.sem, pPr.at(un.v, "pT"))
            dve.wait_ge(pOu.sem, pOu.at(un.v - 2, "out"))
            dst, src = pT_half(un, 1)
            dve.tensor_copy(dst, src).then_inc(*vP.tick("pT"))

        def dve_o(dve, un):
            s = un.k % 4
            dve.wait_ge(pOu.sem, pOu.at(un.v, "out"))
            dve.wait_ge(vR.sem, vR.at(un.v, "recip"))
            dve.wait_ge(pX.sem, pX.at(un.x - 2, "oT"))
            if un.kind is swa:
                for e in range(2):
                    i = dve.tensor_scalar(o_sb[:, un.o_slot, e * DA:(e + 1) * DA], PS[:, 6 + un.par, e * DA:(e + 1) * DA],
                                          sa[:, s, 12 + e:13 + e], None, ALU.mult)
            else:
                e = un.par
                i = dve.tensor_scalar(o_sb[:, un.o_slot, e * VB:(e + 1) * VB], PS[:, 6 + e, 0:VB], sa[:, s, 12:13],
                                      None, ALU.mult)
            i.then_inc(*vO.tick("o"))

        def dve_oT(dve, un):
            if un.last_of_pair:
                dve.wait_ge(aX.sem, aX.at(un.x, "o_hi"))
                kt, col = slice_of(un.kt_out), o_col(un.tile)
                dve.tensor_tensor(H_lo[:, kt, col], PS[:, 6 + un.par, P:2 * P].unsqueeze(1), H_hi[:, kt, col].bitcast(F32),
                                  ALU.subtract).then_inc(*vX.tick("o_lo"))

        def attention_loads(sp):
            sp.wait_ge(va_written, 16 * (NT + 1))
            sp.wait_ge(sw_written, 32 * (NT + 1))
            sp.wait_ge(mq_written, 16 * (NT + 1))
            sp.wait_ge(mk_written, 16 * (NT + 1))
            sp.wait_ge(vb_written, 16 * (NT + 1))
            sp.wait_ge(pads_written, 16 * 4)
            sp.dma_start(sink[:, :], io["swa_sink"][0, :].partition_broadcast(P)).then_inc(att_consts, 16)
            sp.dma_start(mask3[:, :, :], io["mask"]).then_inc(att_consts, 16)

            def window(g, slot):
                if not isinstance(g, int):
                    sp.wait_ge(pOu.sem, pOu.at(g * 4 - 5, "out"))
                sp.dma_start(kk[:, slot, 0:3 * 2 * P].rearrange("p (t c) -> p t c", t=3),
                             scr_ka[bass.ds(g, 3)].rearrange("t p c -> p t c")).then_inc(window_k_landed[slot], 16)
                sp.dma_start(vv[:, slot, 0:3 * P].rearrange("p (t c) -> p t c", t=3),
                             scr_va[bass.ds(g, 3)].rearrange("t p c -> p t c")).then_inc(window_v_landed[slot], 16)

            def block_q(g):
                for k in range(4):
                    sp.wait_ge(pSc.sem, pSc.at(g * 4 + (k - 4), "scores"))
                    sp.dma_start(qa[:, k, :], scr_qa[bass.ds(g, 1), :, k * P:(k + 1) * P].rearrange("a p c -> p (a c)")) \
                      .then_inc(qa_landed[k], 16)

            def head_pair(kind, pair, prev_last):
                n = kind.nk * P
                sp.wait_ge(pOu.sem, pOu.at(prev_last, "out"))
                if kind.kv0 + pair:
                    sp.wait_ge(k_landed, (kind.kv0 + pair) * 16)
                    sp.wait_ge(v_landed, (kind.kv0 + pair) * 16)
                c0 = kind.tile0 * P
                sp.dma_start(kk[0:QKB, pair % 2, 0:2 * n].rearrange("p (h c) -> p h c", h=2),
                             scr_kb[:, 2 * pair:2 * pair + 2, c0:c0 + n]).then_inc(k_landed, 16)
                sp.dma_start(vv[:, pair % 2, 0:n].rearrange("p (t c) -> p t c", t=kind.nk),
                             scr_vb[kind.tile0:kind.tile0 + kind.nk, :, pair * 2 * VB:(pair + 1) * 2 * VB]
                             .rearrange("t p c -> p t c")).then_inc(v_landed, 16)

            def tile_q(kind, pair, i):
                g = i + pair * (kind.nk // 2)
                for e in range(2):
                    sp.wait_ge(pSc.sem, pSc.at(g * 4 + (kind.unit0 + 2 * e + 1 - 4), "scores"))
                    sp.dma_start(qb[0:QKB, e, :, :],
                                 scr_qb[bass.ds(i * 2 + (kind.tile0 + e), 1), :, 2 * pair:2 * pair + 2, :]
                                 .rearrange("a p h c -> p (a h) c")).then_inc(qb_landed[e], 16)

            for g in range(2):
                window(g, g)
                block_q(g)
            with sp.Fori(1, NT // 2) as it:
                for n in range(2):
                    window(it * 2 + n, n)
                    block_q(it * 2 + n)
            order = [(kind, pair) for kind in (mla_p, mla_s) for pair in range(PAIRS)]
            first_unit = [kind.unit0 + pair * 2 * kind.nk for kind, pair in order]
            head_pair(mla_p, 0, first_unit[0] - 5)
            for n, (kind, pair) in enumerate(order):
                tile_q(kind, pair, 0)
                if n + 1 < len(order):
                    head_pair(*order[n + 1], first_unit[n] - 1)
                with sp.Fori(1, kind.nk // 2) as i:
                    tile_q(kind, pair, i)

        def attention_pe(pe):
            pe.wait_ge(mask_ready, 2)
            attention_turns(pe, [(pe_scores, 0), (pe_out, 3), (pe_probs, 2), (pe_turn, 4)])

        def attention_act(act):
            attention_turns(act, [(act_exp, 1), (act_pT, 2), (act_oT, 4)])

        def attention_dve(dve):
            dve.wait_ge(att_consts, 32)
            dve.tensor_copy(ident16[:, :], ident[:, :])
            dve.tensor_copy(mask[:, :, 0, :], mask3[:, 0:1, :].to_broadcast([P, NT, P]))
            dve.tensor_copy(mask[:, :, 1, :], mask3[:, 1:2, :].to_broadcast([P, NT, P])).then_inc(mask_ready, 1)
            dve.wait_ge(mask_ready, 1)
            for first in (0, S_PROMPT // P):
                dve.tensor_copy(mask[:, first, 0, :], mask3[:, 2, :])
            for last in (S_PROMPT // P - 1, NT - 1):
                i = dve.tensor_copy(mask[:, last, 1, :], mask3[:, 2, :])
            i.then_inc(mask_ready, 1)
            attention_turns(dve, [(dve_max, 0), (dve_recip, 1), (dve_o, 3), (dve_pT, 2), (dve_oT, 4)])

        def wo_loads(sp):
            sp.wait_ge(pX.sem, pX.at(NX - 1, "oT"))
            sp.wait_ge(vP.sem, vP.at(NV - 1, "pT"))
            sp.wait_ge(pOu.sem, pOu.at(NV - 1, "out"))
            wo = io["w_out"][0].rearrange("(k p) n -> p k n", p=P)
            with sp.Fori(0, KD // 2) as it:
                for n in range(2):
                    sp.wait_ge(wo_ready, it * 2 + (n + 1))
                    sp.dma_start(raw[:, n, :].rearrange("p (k m) -> p k m", k=KD), wo[:, :, bass.ds((it * 2 + n) * P, P)]) \
                      .then_inc(wo_landed[n], 16)

        def wo_split_hi(act):
            act.wait_ge(pX.sem, pX.at(NX - 1, "oT"))
            act.wait_ge(pOu.sem, pOu.at(NV - 1, "out"))
            with act.Fori(0, KD // 2) as it:
                for n in range(2):
                    act.wait_ge(wo_landed[n], it * 16 + 16)
                    act.wait_ge(wo_done, it * 6 + (3 * n + 3))
                    act.activation(W_hi[:, n, :], raw[:, n, :], ACT.Copy).then_inc(wo_hi, 1)

        def wo_split_lo(pool):
            pool.sem_inc(wo_ready, 2)
            with pool.Fori(0, KD // 2) as it:
                for n in range(2):
                    pool.wait_ge(wo_hi, it * 2 + (n + 1))
                    pool.tensor_tensor(W_lo[:, n, :], raw[:, n, :], W_hi[:, n, :].bitcast(F32), ALU.subtract) \
                        .then_inc(wo_ready, 1)

        def wo_pe(pe):
            pe.wait_ge(vX.sem, vX.at(NX - 1, "o_lo"))
            with pe.Fori(0, KD // 2) as it:
                for n in range(2):
                    pe.wait_ge(wo_ready, it * 2 + (n + 3))
                    for c in range(NCH):
                        pe.wait_ge(wo_added, it * 6 + (3 * n + c + 1))
                        for k in range(KD):
                            w, col = slice(k * P, (k + 1) * P), slice(c * CH, (c + 1) * CH)
                            mm = three_pass(pe, PS[:, 3 * n + c, :], W_hi[:, n, w], W_lo[:, n, w],
                                            H_hi[:, k, col], H_lo[:, k, col], k == 0, k == KD - 1)
                        mm.then_inc(wo_done, 1)

        def wo_dve(dve):
            with dve.Fori(0, KD // 2) as it:
                for n in range(2):
                    for c in range(NCH):
                        dve.wait_ge(wo_done, it * 6 + (3 * n + c + 1 + 6))
                        xt = XT[:, bass.ds(it * 2 + n, 1), c * CH:(c + 1) * CH]
                        dve.scalar_tensor_tensor(out=xt, in0=PS[:, 3 * n + c, :].unsqueeze(1),
                                                 scalar=hgate[:, 1, bass.ds(it * 2 + n, 1), c:c + 1], in1=xt,
                                                 op0=ALU.mult, op1=ALU.add).then_inc(wo_added, 1)

        def last_pe(pe):
            pe.sem_inc(y_turned, 2)
            with pe.Fori(0, NT // 2) as it:
                for n in range(2):
                    pe.wait_ge(x_staged, it * 2 + (n + 1))
                    pe.wait_ge(y_scaled, it * 2 + (n + 1))
                    for k in range(KD):
                        mm = pe.transpose(PS[:, 2 * n + k // 4, (k % 4) * P:(k % 4 + 1) * P], x_out[:, n, k, :], ident[:, :])
                    mm.then_inc(y_turned, 1)

        def last_act(act):
            with act.Fori(0, NT // 2) as it:
                for n in range(2):
                    act.wait_ge(y_turned, it * 2 + (n + 3))
                    act.wait_ge(y_scaled, it * 2 + (n + 1))
                    act.activation(y_sq[:, :], PS[:, 2 * n:2 * n + 2, :].rearrange("p b c -> p (b c)"), ACT.Square,
                                   accum_out=y_st[:, n, 0:1]).then_inc(y_summed, 1)
                    act.wait_ge(y_summed, it * 2 + (n + 1))
                    act.activation(y_st[:, n, 1:2], y_st[:, n, 0:1], ACT.Sqrt, bias=eps_col[:, 0:1], scale=1.0 / D) \
                       .then_inc(y_root, 1)

        def last_dve(dve):
            dve.sem_inc(y_scaled, 2)
            dve.wait_ge(fgain_landed, 16)
            with dve.Fori(0, NT // 2) as it:
                for n in range(2):
                    dve.wait_ge(y_turned, it * 2 + (n + 1))
                    dve.tensor_copy(x_out[:, n, :, :], XT[:, :, bass.ds((it * 2 + n) * P, P)]).then_inc(x_staged, 1)
                for n in range(2):
                    dve.wait_ge(y_root, it * 2 + (n + 1))
                    dve.reciprocal(y_st[:, n, 1:2], y_st[:, n, 1:2]).then_inc(y_rstd, 1)
                    dve.wait_ge(y_rstd, it * 2 + (n + 1))
                    dve.wait_ge(y_written[n], it * 16 + 16)
                    dve.scalar_tensor_tensor(out=y_sb[:, n, :], in0=PS[:, 2 * n:2 * n + 2, :].rearrange("p b c -> p (b c)"),
                                             scalar=y_st[:, n, 1:2], in1=fgain[:, :], op0=ALU.mult, op1=ALU.mult) \
                       .then_inc(y_scaled, 1)

        def last_dma(sp):
            sp.wait_ge(acc_done, DS + 2 * NPAIR * NCH * KD)
            sp.dma_start(fgain[:, :], io["final_norm"][0, :].partition_broadcast(P)).then_inc(fgain_landed, 16)
            sp.sem_inc(y_written[0], 16)
            sp.sem_inc(y_written[1], 16)
            for y, first, tiles in ((io["y_prompt"], 0, S_PROMPT // P), (io["y_sample"], S_PROMPT // P, S_SAMPLE // P)):
                with sp.Fori(0, tiles // 2) as it:
                    for n in range(2):
                        sp.wait_ge(y_scaled, it * 2 + (first + n + 3))
                        sp.dma_start(y[0, bass.ds((it * 2 + n) * P, P), :], y_sb[:, n, :]).then_inc(y_written[n], 16)
            for n in range(2):
                sp.wait_ge(y_written[n], 16 + 16 * NT // 2)

        @block.sync
        def _(sp):
            sp.sem_inc(va_written, 16)
            sp.sem_inc(sw_written, 32)
            sp.sem_inc(vb_written, 16)
            sp.sem_inc(mq_written, 16)
            sp.sem_inc(mk_written, 16)
            start_loads(sp)
            ffn_loads(sp, 0)
            mix_weight_loads(sp)
            mix_dma(sp)
            attention_loads(sp)
            wo_loads(sp)
            sp.wait_ge(wo_ready, KD + 2)
            ffn_loads(sp, 1)
            last_dma(sp)

        @block.tensor
        def _(pe):
            start_counts(pe, "pe")
            pe.sem_inc(wo_done, 6)
            start_pe(pe)
            norm_pe(pe, 0)
            ffn_pe(pe, 0)
            mix_pe(pe)
            attention_pe(pe)
            wo_pe(pe)
            norm_pe(pe, 1)
            ffn_pe(pe, 1)
            last_pe(pe)

        @block.scalar
        def _(act):
            start_counts(act, "act")
            start_act(act)
            norm_act(act, 0)
            ffn_act(act, 0)
            mix_weight_hi(act)
            mix_act(act)
            attention_act(act)
            wo_split_hi(act)
            act.wait_ge(wo_done, 6 + KD * NCH)
            act.wait_ge(wo_added, 6 + KD * NCH)
            norm_act(act, 1)
            ffn_act(act, 1)
            last_act(act)

        @block.vector
        def _(dve):
            start_counts(dve, "dve")
            dve.sem_inc(wo_added, 6)
            start_dve(dve)
            norm_dve(dve, 0)
            ffn_dve(dve, 0)
            mix_dve(dve)
            attention_dve(dve)
            wo_dve(dve)
            norm_dve(dve, 1)
            ffn_dve(dve, 1)
            last_dve(dve)

        @block.gpsimd
        def _(pool):
            start_counts(pool, "pool")
            pool.sem_inc(w_ready, RS)
            ffn_split_lo(pool, 0)
            mix_weight_lo(pool)
            mix_pool(pool)
            wo_split_lo(pool)
            ffn_split_lo(pool, 1)


INPUTS = ["x_prompt", "x_sample", "c_prompt", "c_sample", "ada_w", "ada_b", "ffn1_norm", "ffn1_wg", "ffn1_wu",
          "ffn1_wd", "mix_norm", "w_in", "swa_q_norm", "swa_k_norm", "swa_sink", "mla_q_lora_norm", "mla_w_uq",
          "mla_kv_lora_norm", "mla_w_ukv", "mla_q_norm", "mla_k_norm", "w_out", "ffn2_norm", "ffn2_wg", "ffn2_wu",
          "ffn2_wd", "final_norm"]


def shape_constants():
    out = {"ident": np.eye(P, dtype=np.float32)}
    pos = np.concatenate([np.arange(S_PROMPT), np.arange(S_SAMPLE)]).astype(np.float32)
    tabs = []
    for d in (DA, ROPE):
        inv = (np.float32(10000.0) ** (-np.arange(0, d, 2, dtype=np.float32) / np.float32(d))).astype(np.float32)
        ang = (pos[:, None] * inv[None, :]).astype(np.float32)
        cs, sn = np.cos(ang).astype(np.float32), np.sin(ang).astype(np.float32)
        tabs += [cs, cs, -sn, sn]
    out["rope"] = np.concatenate(tabs, axis=1).reshape(NT, P, 2 * DA + 2 * ROPE)
    q, k = np.arange(P)[:, None], np.arange(P)[None, :]
    out["mask"] = np.stack([np.where(k >= q, 0.0, -1e30), np.where(k <= q, 0.0, -1e30), np.full((P, P), -1e30)],
                           axis=1).astype(np.float32)
    return out


def kernel(**inputs):
    import concourse.bacc as bacc
    from concourse.bass_utils import run_bass_kernel_spmd as run

    nc = bacc.Bacc("TRN2", target_bir_lowering=False, num_devices=1)
    arrays, io = {}, {}

    def given(name, a):
        arrays[f"in_{name}"] = a
        io[name] = nc.dram_tensor(f"in_{name}", a.shape, mybir.dt.from_np(a.dtype), kind="ExternalInput").ap()

    for name in INPUTS:
        given(name, np.ascontiguousarray(inputs[name]))
    for name, a in shape_constants().items():
        given(name, a)
    for name, s in (("y_prompt", S_PROMPT), ("y_sample", S_SAMPLE)):
        io[name] = nc.dram_tensor(f"out_{name}", (1, s, D), F32, kind="ExternalOutput").ap()
    build(nc, io)
    r = run(nc, [arrays], core_ids=[0])
    return r.results[0]["out_y_prompt"], r.results[0]["out_y_sample"]
```
